# Optimizing a Trainium2 kernel written in Bass

```python
import math
import jax, jax.numpy as jnp
from jax import lax
import numpy as np

D_MODEL = 1024
BATCH = 1
SEQ = 256
DEPTH = 2

N_HEADS = 16
HEAD_DIM = D_MODEL // N_HEADS
ATTN_W = N_HEADS * HEAD_DIM
DIL_PAIRS = ((128, 1), (512, 4), (2048, 16))
N_DIL = len(DIL_PAIRS)
BLOCK = 128
KV_RANK = 256
N_IDX_HEADS = 8
IDX_DIM = 64
TOPK_MAX = 256
N_MEM = 256
N_CROSS_HEADS = 4
CROSS_HEAD_DIM = 64
CROSS_WIDTH = N_CROSS_HEADS * CROSS_HEAD_DIM
REL_BUCKETS = 32
REL_MAX_DIST = 2048
D_FF_DENSE = 2816
N_EXPERTS = 8
TOP_K_EXPERTS = 2
D_FF_EXPERT = 3584
RMS_EPS = 1e-6
NEG_INF = -1e30
A_IN = N_DIL * ATTN_W + 2 * ATTN_W + CROSS_WIDTH
B_IN = ATTN_W + KV_RANK + N_IDX_HEADS * IDX_DIM + IDX_DIM + N_IDX_HEADS + CROSS_WIDTH
OUT_IN = ATTN_W + CROSS_WIDTH
N_EVEN = (DEPTH + 1) // 2
N_ODD = DEPTH // 2

kernel_name = "hybrid_dilated_dsa_moe_decoder"

def rmsnorm(x, g):
    xf = x.astype(jnp.float32)
    y = xf * lax.rsqrt(jnp.mean(xf * xf, axis=-1, keepdims=True) + RMS_EPS)
    return (y * g.astype(jnp.float32)).astype(x.dtype)

def split_cols(t, sizes):
    offs = np.cumsum(np.array(sizes))[:-1].tolist()
    return jnp.split(t, offs, axis=-1)

def rel_bucket(dist):
    n = jnp.maximum(dist, 0)
    max_exact = REL_BUCKETS // 2
    nf = jnp.maximum(n, 1).astype(jnp.float32)
    large = max_exact + (jnp.log(nf / max_exact) / math.log(REL_MAX_DIST / max_exact)
                         * (REL_BUCKETS - max_exact)).astype(jnp.int32)
    large = jnp.minimum(large, REL_BUCKETS - 1)
    return jnp.where(n < max_exact, n, large)

def dilated_branch(q, k, v, rel_bias, window, dilation):
    B, S, H, hd = q.shape
    L = S // dilation
    Lp = -(-L // BLOCK) * BLOCK
    nb = Lp // BLOCK
    span = window // dilation

    def to_sub(t):
        t = t.reshape(B, L, dilation, H, hd).transpose(0, 2, 1, 3, 4)
        t = jnp.pad(t, ((0, 0), (0, 0), (0, Lp - L), (0, 0), (0, 0)))
        return t.reshape(B, dilation, nb, BLOCK, H, hd)

    def with_prev(t):
        prev = jnp.pad(t, ((0, 0), (0, 0), (1, 0), (0, 0), (0, 0), (0, 0)))[:, :, :-1]
        return jnp.concatenate([prev, t], axis=3)

    qs = to_sub(q)
    kk = with_prev(to_sub(k))
    vv = with_prev(to_sub(v))
    scores = jnp.einsum('bdnqhc,bdnkhc->bdnhqk', qs, kk,
                        preferred_element_type=jnp.float32) * (hd ** -0.5)
    qi = jnp.arange(BLOCK)[:, None]
    ki = jnp.arange(2 * BLOCK)[None, :]
    rel = qi + BLOCK - ki
    bias = jnp.moveaxis(rel_bias[rel_bucket(rel * dilation)], -1, 0).astype(jnp.float32)
    kpos = jnp.arange(nb)[:, None, None] * BLOCK + ki[None] - BLOCK
    allowed = (rel[None] >= 0) & (rel[None] <= span) & (kpos >= 0)
    scores = jnp.where(allowed[:, None], scores + bias, NEG_INF)
    m = jnp.max(scores, axis=-1)
    p = jnp.exp(scores - m[..., None])
    l = jnp.sum(p, axis=-1)
    o = jnp.einsum('bdnhqk,bdnkhc->bdnqhc', p, vv.astype(jnp.float32))

    def from_sub(t):
        t = t.reshape((B, dilation, Lp) + t.shape[4:])[:, :, :L]
        return jnp.swapaxes(t, 1, 2).reshape((B, S) + t.shape[3:])

    return (from_sub(o), from_sub(jnp.swapaxes(m, -1, -2)), from_sub(jnp.swapaxes(l, -1, -2)))

def mixer_dilated(q_groups, k, v, rel_bias):
    B, S, _ = k.shape
    heads = lambda t: t.reshape(B, S, N_HEADS, HEAD_DIM)
    kh, vh = heads(k), heads(v)
    branches = [dilated_branch(heads(qg), kh, vh, rel_bias, w, d)
                for qg, (w, d) in zip(q_groups, DIL_PAIRS)]
    m_max = jnp.max(jnp.stack([b[1] for b in branches]), axis=0)
    num = jnp.zeros_like(branches[0][0])
    den = jnp.zeros_like(m_max)
    for o_g, m_g, l_g in branches:
        a = jnp.exp(m_g - m_max)
        num = num + a[..., None] * o_g
        den = den + a * l_g
    return (num / den[..., None]).astype(k.dtype).reshape(B, S, ATTN_W)

def mixer_dsa(q, c_kv, q_idx, k_idx, w_idx, w_uk, w_uv, rel_bias):
    B, S, _ = q.shape
    topk = min(TOPK_MAX, S // 4)
    nb = S // BLOCK
    qh = q.reshape(B, S, N_HEADS, HEAD_DIM)
    q_lat = jnp.einsum('bshc,rhc->bshr', qh, w_uk)
    q_idx = q_idx.reshape(B, S, N_IDX_HEADS, IDX_DIM)
    k_idx_f = k_idx.astype(jnp.float32)

    def blockify(t):
        return jnp.moveaxis(t.reshape((B, nb, BLOCK) + t.shape[2:]), 1, 0)

    def one_block(args):
        i, ql, qib, wib = args
        s = jnp.einsum('bqhc,bsc->bqhs', qib.astype(jnp.float32), k_idx_f) * (IDX_DIM ** -0.5)
        score = jnp.einsum('bqh,bqhs->bqs', wib.astype(jnp.float32) * (N_IDX_HEADS ** -0.5),
                           jax.nn.relu(s))
        tpos = i * BLOCK + jnp.arange(BLOCK)
        causal = jnp.arange(S)[None, :] <= tpos[:, None]
        score = jnp.where(causal[None], score, NEG_INF)
        _, idx = lax.top_k(score, topk)
        valid = idx <= tpos[None, :, None]
        c_sel = jax.vmap(lambda c, ix: c[ix])(c_kv, idx)
        logits = jnp.einsum('bqhr,bqkr->bhqk', ql, c_sel,
                            preferred_element_type=jnp.float32) * (HEAD_DIM ** -0.5)
        bias = rel_bias[rel_bucket(tpos[None, :, None] - idx)]
        logits = logits + jnp.moveaxis(bias, -1, 1).astype(jnp.float32)
        logits = jnp.where(valid[:, None], logits, NEG_INF)
        p = jax.nn.softmax(logits, axis=-1)
        o_lat = jnp.einsum('bhqk,bqkr->bqhr', p, c_sel.astype(jnp.float32))
        return o_lat.astype(q.dtype)

    o_lat = lax.map(one_block, (jnp.arange(nb), blockify(q_lat), blockify(q_idx), blockify(w_idx)))
    o_lat = jnp.moveaxis(o_lat, 0, 1).reshape(B, S, N_HEADS, KV_RANK)
    o = jnp.einsum('bshr,rhc->bshc', o_lat, w_uv)
    return o.reshape(B, S, ATTN_W)

def cross_attention(qc, mem_n, w_mem_kv):
    B, S, _ = qc.shape
    kv = jnp.einsum('bnd,de->bne', mem_n, w_mem_kv)
    k, v = jnp.split(kv, 2, axis=-1)
    k = k.reshape(B, N_MEM, N_CROSS_HEADS, CROSS_HEAD_DIM)
    v = v.reshape(B, N_MEM, N_CROSS_HEADS, CROSS_HEAD_DIM)
    q = qc.reshape(B, S, N_CROSS_HEADS, CROSS_HEAD_DIM)
    logits = jnp.einsum('bshc,bnhc->bhsn', q, k,
                        preferred_element_type=jnp.float32) * (CROSS_HEAD_DIM ** -0.5)
    p = jax.nn.softmax(logits, axis=-1)
    o = jnp.einsum('bhsn,bnhc->bshc', p, v.astype(jnp.float32))
    return o.astype(qc.dtype).reshape(B, S, CROSS_WIDTH)

def swiglu(h, w_gate, w_up, w_down):
    return (jax.nn.silu(h @ w_gate) * (h @ w_up)) @ w_down

def moe_swiglu(h, w_router, w_gate, w_up, w_down):
    B, S, D = h.shape
    t = h.reshape(B * S, D)
    logits = (t @ w_router).astype(jnp.float32)
    top_val, top_idx = lax.top_k(logits, TOP_K_EXPERTS)
    gate_top = jax.nn.softmax(top_val, axis=-1)
    gates = jnp.sum(jax.nn.one_hot(top_idx, N_EXPERTS, dtype=jnp.float32) * gate_top[..., None], axis=1)
    y = jnp.zeros((B * S, D), jnp.float32)
    for e in range(N_EXPERTS):
        y = y + gates[:, e:e + 1] * swiglu(t, w_gate[e], w_up[e], w_down[e]).astype(jnp.float32)
    return y.astype(h.dtype).reshape(B, S, D)

def setup_inputs(seed: int = 0) -> dict:
    key = jax.random.key(seed)
    ks = iter(jax.random.split(key, 32))
    nrm = lambda shape, fan_in: jax.random.normal(next(ks), shape, jnp.float32) * (fan_in ** -0.5)
    gain = lambda shape: 1.0 + 0.02 * jax.random.normal(next(ks), shape, jnp.float32)
    D = D_MODEL
    return {
        "x": jax.random.normal(next(ks), (BATCH, SEQ, D), jnp.float32),
        "mem": jax.random.normal(next(ks), (BATCH, N_MEM, D), jnp.float32),
        "rel_bias": 0.2 * jax.random.normal(next(ks), (REL_BUCKETS, N_HEADS), jnp.float32),
        "mem_norm": gain((D,)),
        "final_norm": gain((D,)),
        "mixer_norm": gain((DEPTH, D)),
        "ffn_norm": gain((DEPTH, D)),
        "w_mem_kv": nrm((DEPTH, D, 2 * CROSS_WIDTH), D),
        "w_out": nrm((DEPTH, OUT_IN, D), OUT_IN),
        "even_w_in": nrm((N_EVEN, D, A_IN), D),
        "even_w_gate": nrm((N_EVEN, D, D_FF_DENSE), D),
        "even_w_up": nrm((N_EVEN, D, D_FF_DENSE), D),
        "even_w_down": nrm((N_EVEN, D_FF_DENSE, D), D_FF_DENSE),
        "odd_w_in": nrm((N_ODD, D, B_IN), D),
        "odd_kv_norm": gain((N_ODD, KV_RANK)),
        "odd_w_uk": nrm((N_ODD, KV_RANK, N_HEADS, HEAD_DIM), KV_RANK),
        "odd_w_uv": nrm((N_ODD, KV_RANK, N_HEADS, HEAD_DIM), KV_RANK),
        "odd_w_router": nrm((N_ODD, D, N_EXPERTS), D),
        "odd_w_gate": nrm((N_ODD, N_EXPERTS, D, D_FF_EXPERT), D),
        "odd_w_up": nrm((N_ODD, N_EXPERTS, D, D_FF_EXPERT), D),
        "odd_w_down": nrm((N_ODD, N_EXPERTS, D_FF_EXPERT, D), D_FF_EXPERT),
    }

def reference(x, mem, rel_bias, mem_norm, final_norm, mixer_norm, ffn_norm, w_mem_kv, w_out,
              even_w_in, even_w_gate, even_w_up, even_w_down,
              odd_w_in, odd_kv_norm, odd_w_uk, odd_w_uv,
              odd_w_router, odd_w_gate, odd_w_up, odd_w_down):
    mem_n = rmsnorm(mem, mem_norm)
    for i in range(DEPTH):
        j = i // 2
        h = rmsnorm(x, mixer_norm[i])
        if i % 2 == 0:
            parts = split_cols(h @ even_w_in[j], [ATTN_W] * N_DIL + [ATTN_W, ATTN_W, CROSS_WIDTH])
            mix = mixer_dilated(parts[:N_DIL], parts[N_DIL], parts[N_DIL + 1], rel_bias)
            qc = parts[N_DIL + 2]
        else:
            q, c_kv, q_idx, k_idx, w_idx, qc = split_cols(
                h @ odd_w_in[j],
                [ATTN_W, KV_RANK, N_IDX_HEADS * IDX_DIM, IDX_DIM, N_IDX_HEADS, CROSS_WIDTH])
            c_kv = rmsnorm(c_kv, odd_kv_norm[j])
            mix = mixer_dsa(q, c_kv, q_idx, k_idx, w_idx, odd_w_uk[j], odd_w_uv[j], rel_bias)
        cross = cross_attention(qc, mem_n, w_mem_kv[i])
        x = x + jnp.concatenate([mix, cross], axis=-1) @ w_out[i]
        h = rmsnorm(x, ffn_norm[i])
        if i % 2 == 0:
            x = x + swiglu(h, even_w_gate[j], even_w_up[j], even_w_down[j])
        else:
            x = x + moe_swiglu(h, odd_w_router[j], odd_w_gate[j], odd_w_up[j], odd_w_down[j])
    return rmsnorm(x, final_norm)


_drawn_inputs = setup_inputs


def setup_inputs(seed=0):
    import zlib

    import numpy as np

    out = dict(_drawn_inputs(seed))
    spreads = {}
    factors = {'mem_norm': 4.842, 'final_norm': 2.879, 'odd_kv_norm': 3.261}
    for name, (base, spread) in spreads.items():
        noise = np.random.default_rng([zlib.crc32(name.encode()), seed]).standard_normal(out[name].shape)
        drawn = base * np.exp(spread * noise) if base else spread * noise
        out[name] = __import__('jax').numpy.asarray(drawn.astype(out[name].dtype))
    for name, factor in factors.items():
        out[name] = (out[name] * factor).astype(out[name].dtype)
    return out
```

```python
import math
from contextlib import ExitStack

import numpy as np

import concourse.bass as bass
from concourse import mybir

F32 = mybir.dt.float32
F32R = mybir.dt.float32r
I32 = mybir.dt.int32
U32 = mybir.dt.uint32
ALU = mybir.AluOpType
ACT = mybir.ActivationFunctionType
AX_X = mybir.AxisListType.X

P = 128
D = 1024
DC = D // P
SEQ = 256
TT = SEQ // P
HEADS, HD = 16, 64
PAIRS = HEADS // 2
XPAIRS = 2
NPAIR = PAIRS + XPAIRS
SCALE = HD ** -0.5
EPS = 1e-6
NEG = -1e30
TAKEN = -3e38
NBR = 3
DIL = ((128, 1), (512, 4), (2048, 16))
BUCKETS, MAX_DIST = 32, 2048
RANK = 256
RC = RANK // P
IDX_HEADS = 8
TOPK = min(256, SEQ // 4)
FF = 2816
FC = FF // P
EXPERTS = 8
FE = 3584
FT = 512
NT = FE // FT
CAP = 128
EXTRA = 2 * SEQ // (CAP + 1)
NPASS = EXPERTS + EXTRA
COLS = NPASS + 1
RING = 7
UNIT = 1024
HALF = 2 * UNIT
SLOTS = 6
CAUSAL = P + SEQ

C_ID, C_MASK, C_TRI, C_ONES, C_IOTA, C_HOT = 0, 128, 1152, 1280, 1408, 1536
C_N = C_HOT + 384
G_MEM, G_MIX0, G_FFN0, G_MIX1, G_FFN1, G_KV, G_N = 0, 8, 16, 24, 32, 40, 42


def distance_buckets(n):
    half = BUCKETS // 2
    nf = np.maximum(n, 1).astype(np.float32)
    large = half + (np.log(nf / np.float32(half)) / np.float32(math.log(MAX_DIST / half))
                    * np.float32(BUCKETS - half)).astype(np.int32)
    return np.where(n < half, n, np.minimum(large, BUCKETS - 1))


def shape_constants():
    c = np.zeros((P, C_N), np.float32)
    row, col = np.arange(P)[:, None], np.arange(P)[None, :]
    c[:, C_ID:C_ID + P] = row == col
    dist = P + row - np.arange(2 * P)[None, :]
    for b, (window, dilation) in enumerate(DIL):
        seen = (dist >= 0) & (dist <= window) & (dist % dilation == 0)
        c[:, C_MASK + b * 256:C_MASK + (b + 1) * 256] = np.where(seen, 0.0, NEG)
    c[:, C_MASK + 768:C_MASK + 1024] = np.where(dist >= 0, 0.0, NEG)
    c[:, C_TRI:C_TRI + P] = row < col
    c[:, C_ONES:C_ONES + P] = 1.0
    c[:, C_IOTA:C_IOTA + P] = col
    back = np.maximum(255 - np.arange(384), 0)
    c[:BUCKETS, C_HOT:C_HOT + 384] = distance_buckets(back)[None, :] == np.arange(BUCKETS)[:, None]
    return c


ORDER = [("gate", 0), ("up", 0)]
for _j in range(1, NT):
    ORDER += [("gate", _j), ("up", _j), ("down", _j - 1)]
ORDER.append(("down", NT - 1))
TILES = len(ORDER)
PASS_UNITS = 4 * TILES

FFN = [("gate", 0), ("up", 0)]
for _c in range(1, FC):
    FFN += [("gate", _c), ("up", _c), ("down", _c - 1)]
FFN.append(("down", FC - 1))
FFN_LOOPS = (FC - 2) // 2


class Units:

    def __init__(self):
        self.slot, self.previous, self.loads, self.at = [], [], [], {}
        last, loaded = [None] * SLOTS, [0] * SLOTS

        def add(key, slot, loads=1):
            self.at[key] = len(self.slot)
            loaded[slot] += loads
            self.previous.append(last[slot])
            self.loads.append(loaded[slot])
            last[slot] = len(self.slot)
            self.slot.append(slot)
        for n in range(8):
            add(("mem", n), n % SLOTS)
        for l in range(2):
            for g in range(PAIRS):
                for m in range((NBR + 2, 3)[l]):
                    add(("pair", l, g, m), m if l == 0 else 3 * (g % 2) + m)
            for j in range(XPAIRS):
                add(("pair", l, PAIRS + j, 0), (5, 0)[j] if l == 0 else j)
            for ch in range(NPAIR):
                add(("out", l, ch), (ch + 1 + l) % SLOTS)
            if l == 0:
                for n in range(len(FFN)):
                    add(("ffn", n), n % SLOTS)
                for n in range(7):
                    add(("idx", n), n % SLOTS, 2 if n == 6 else 1)
        self.count = len(self.slot)


U = Units()
BASE = U.count
assert all(U.slot[BASE - SLOTS + u] == u for u in range(SLOTS)) and PASS_UNITS % SLOTS == 0


def along(i, first, values):
    if isinstance(i, int):
        return values[i - first]
    step = values[1] - values[0]
    assert all(b - a == step for a, b in zip(values, values[1:]))
    return i * step + (values[0] - first * step)


class Pair:

    def __init__(self, l, idx, par, span=None):
        self.l, self.idx, self.par = l, idx, par
        self.span = [idx] if span is None else list(span)
        self.g = 2 * idx + par
        gs = [2 * i + par for i in self.span]
        self.cross = gs[0] >= PAIRS
        self.nbr = 1 if self.cross or l else NBR
        self.kind = "cross" if self.cross else ("even", "odd")[l]
        self.mats = 1 if self.cross else self.nbr + 2
        self.gs = gs

    def value(self, f):
        return along(self.idx, self.span[0], [f(g) for g in self.gs])

    def unit(self, m):
        return [U.at[("pair", self.l, g, m)] for g in self.gs]

    def before(self):
        full = (NBR + 2, 3)[self.l]
        return self.value(lambda g: full * g if g <= PAIRS else full * PAIRS + g - PAIRS)

    def bank(self, m):
        full = (NBR + 2, 3)[self.l]
        g = self.gs[0]
        return 3 + ((full * g if g <= PAIRS else full * PAIRS + g - PAIRS) + m) % 2


def pair_at(l, g):
    return Pair(l, g // 2, g % 2)


def steps(l, engine, one):
    last = PAIRS // 2 - 3
    span = range(0, last + 1)
    with engine.Fori(0, last + 1) as i:
        for par in range(2):
            now = Pair(l, i, par, span)
            nxt = Pair(l, i + (par + 1) // 2, (par + 1) % 2, [k + (par + 1) // 2 for k in span])
            aft = Pair(l, i + 1, par, [k + 1 for k in span])
            one(now, nxt, aft)
    for g in range(2 * (last + 1), NPAIR):
        one(pair_at(l, g), *(pair_at(l, h) if h < NPAIR else None for h in (g + 1, g + 2)))


def build(nc, x, mem, rel_bias, gains, final_norm, consts, w_mem_kv, w_out, even_w_in, even_w_gate,
          even_w_up, even_w_down, odd_w_in, odd_w_uk, odd_w_uv, odd_w_router, odd_w_gate, odd_w_up,
          odd_w_down, out):
    scratch = nc.dram_tensor("bias_rows", [P, HEADS, 384], F32, kind="Internal").ap()

    def rows(w):
        return w.rearrange("(c p) n -> p c n", p=P)

    w_in = (rows(even_w_in[0]), rows(odd_w_in[0]))
    w_kv = (rows(w_mem_kv[0]), rows(w_mem_kv[1]))
    w_o = (rows(w_out[0]), rows(w_out[1]))
    w_uk = rows(odd_w_uk[0].rearrange("r h c -> r (h c)"))
    w_uv = rows(odd_w_uv[0].rearrange("r h c -> r (h c)"))
    ffn_w = {"gate": rows(even_w_gate[0]), "up": rows(even_w_up[0]), "down": rows(even_w_down[0])}
    w_router = rows(odd_w_router[0])
    expert_w = {"gate": odd_w_gate[0].rearrange("e (c p) f -> p (e c) f", p=P),
                "up": odd_w_up[0].rearrange("e (c p) f -> p (e c) f", p=P),
                "down": odd_w_down[0].rearrange("e (c p) n -> p (e c) n", p=P)}
    x_d = x[0].rearrange("(t p) d -> p t d", p=P)
    mem_d = mem[0].rearrange("(t p) d -> p t d", p=P)
    out_d = out[0].rearrange("(t p) d -> p t d", p=P)
    Q_X = (NBR + 2) * D
    O_C, O_QI = D, D + RANK
    O_KI = O_QI + IDX_HEADS * HD
    O_WI = O_KI + HD
    O_X = O_WI + IDX_HEADS

    with ExitStack() as ctx:
        def sb(name, shape, dt=F32):
            return ctx.enter_context(nc.sbuf_tensor(name, shape, dt))

        def sem(name):
            return ctx.enter_context(nc.semaphore(name))

        ps = ctx.enter_context(nc.psum_tensor("ps", [P, 8, 512], F32))
        big = sb("big", [P, RING * HALF])
        raw = [big[:, s * UNIT:(s + 1) * UNIT] for s in range(SLOTS)]
        bmp = big[:, 6144:9216].rearrange("p (r h b s) -> p r h b s", r=2, h=2, b=NBR)
        bias = big[:, 9216:13312].rearrange("p (h s) -> p h s", h=HEADS)
        ring = [big[:, s * HALF:(s + 1) * HALF] for s in range(RING)]
        w_hi = sb("w_hi", [P, SLOTS, UNIT], F32R)
        w_lo = sb("w_lo", [P, SLOTS, UNIT], F32R)
        X = sb("X", [P, TT, D])
        XH = sb("XH", [P, TT, D])
        h_hi = sb("h_hi", [P, DC, SEQ], F32R)
        h_lo = sb("h_lo", [P, DC, SEQ], F32R)
        m_hi = sb("m_hi", [P, NPAIR, SEQ], F32R)
        m_lo = sb("m_lo", [P, NPAIR, SEQ], F32R)
        con = sb("con", [P, C_N])
        gn = sb("gn", [P, G_N])
        relb = sb("relb", [BUCKETS, HEADS])
        z = sb("z", [P, NBR * CAUSAL])
        pr = sb("pr", [P, NBR * CAUSAL])
        tmp = sb("tmp", [P, CAUSAL])
        pn = sb("pn", [P, 512])
        pts = sb("pts", [P, 512])
        qT = sb("qT", [P, 2, NBR, SEQ])
        kT = sb("kT", [P, 2, SEQ])
        vT = sb("vT", [P, SEQ])
        vN = sb("vN", [P, TT, P])
        kx = sb("kx", [P, 2 * XPAIRS, SEQ])
        vx = sb("vx", [P, 2 * XPAIRS, TT, P])
        small = sb("small", [P, 64])
        qiT = sb("qiT", [P, 4, SEQ])
        kiT = sb("kiT", [P, SEQ])
        c_hi = sb("c_hi", [P, RC, SEQ], F32R)
        c_lo = sb("c_lo", [P, RC, SEQ], F32R)
        selm = sb("selm", [P, CAUSAL])
        rt = selm
        wr = kT[:, 0, 0:DC * EXPERTS].rearrange("p (c n) -> p c n", c=DC)
        wwi = big[:, 13312:13312 + DC * IDX_HEADS].rearrange("p (c n) -> p c n", c=DC)
        itab = sb("itab", [P, 4], I32)
        uidx = sb("uidx", [P, TT, 8], U32)

        ebuf = qT[0:HEADS, :, :, :].rearrange("h r b n -> h (r b n)")[:, 0:384]
        ident = con[:, C_ID:C_ID + P]
        tri = con[:, C_TRI:C_TRI + P]
        ones = con[:, C_ONES:C_ONES + P]
        iota = con[:, C_IOTA:C_IOTA + P]
        iota8 = con[:, C_IOTA:C_IOTA + 8]
        causal = con[:, C_MASK + 768:C_MASK + 1024]
        ss, ms, sd, rstd = (small[:, i:i + 2] for i in (0, 2, 4, 6))
        nmx, den, rden = (small[:, i:i + 2] for i in (8, 10, 12))
        ms8 = small[:, 16:32].rearrange("p (t k) -> p t k", t=2)
        wis = small[:, 32:48].rearrange("p (t k) -> p t k", t=2)
        cN = pn[:, :].rearrange("p (t r) -> p t r", t=TT)
        rl = z[:, 0:2 * CAUSAL].rearrange("p (r s) -> p r s", r=2)
        scr = pr[:, 0:2 * CAUSAL].rearrange("p (r s) -> p r s", r=2)
        fsg = z[:, 0:512].rearrange("p (r n) -> p r n", r=2)
        fh = pr[:, 0:512].rearrange("p (r n) -> p r n", r=2)
        f_hi, f_lo = c_hi, c_lo
        esg, eh = qT[:, 0, 0:2, :].rearrange("p b n -> p (b n)"), pts[:, :]
        e_hi = h_hi[:, 0:2, :].rearrange("p c n -> p (c n)").rearrange("p (k n) -> p k n", k=4)
        e_lo = h_lo[:, 0:2, :].rearrange("p c n -> p (c n)").rearrange("p (k n) -> p k n", k=4)
        g_hi = m_hi[:, 0:4, :].rearrange("p c n -> p (c n)").rearrange("p (c n) -> p c n", c=DC)
        g_lo = m_lo[:, 0:4, :].rearrange("p c n -> p (c n)").rearrange("p (c n) -> p c n", c=DC)
        ysb = z[:, 0:D]
        fin_gain = qiT[:, :, :].rearrange("p c n -> p (c n)")
        Sg = pn[:, 0:256].rearrange("p (t s) -> p t s", t=TT)
        SG = pn[:, 256:512].rearrange("p (t s) -> p t s", t=TT)
        SGT = kiT[:, :]
        lg, sel, gate_e, oh0, oh1 = (rt[:, i:i + 16].rearrange("p (t k) -> p t k", t=2)
                                     for i in (0, 16, 32, 48, 64))
        top8 = rt[:, 80:96].rearrange("p (t k) -> p t k", t=2)
        idxf = rt[:, 96:112].rearrange("p (t k) -> p t k", t=2)
        slot1 = rt[:, 112:128].rearrange("p (t k) -> p t k", t=2)
        slotc = rt[:, 128:152].rearrange("p (t k) -> p t k", t=2)
        gatec = rt[:, 152:176].rearrange("p (t k) -> p t k", t=2)
        dlt, ex2, den2, g1, g2 = (rt[:, i:i + 2] for i in (176, 178, 180, 182, 184))
        over, pa, pb, pc = (rt[:, i:i + 8] for i in (192, 200, 208, 216))
        ind = rt[:, 224:248].rearrange("p (k e) -> p k e", k=EXTRA)
        junk8 = rt[:, 248:256]
        tabf = rt[:, 256:260]

        s_x, s_con, s_mem, s_rel, s_wr, s_ww = map(
            sem, ("x_in", "consts_in", "mem_in", "rel_in", "router_in", "idx_weights_in"))
        s_e, s_eb, s_scrw, s_bias, s_bm = map(sem, ("rel_rows", "rel_rows_sb", "rows_out", "bias_in", "bias_masked"))
        s_ss, s_ms, s_sd, s_rstd, s_xh, s_ntr, s_nhi, s_nlo = map(
            sem, ("sum_squares", "mean_square", "root", "rstd", "normalised", "norm_turned", "norm_hi", "norm_lo"))
        s_xr = sem("residual_added")
        s_raw = [sem(f"raw_in{s}") for s in range(SLOTS)]
        s_hi, s_lo, s_used = map(sem, ("unit_hi", "unit_lo", "unit_used"))
        names = ("evacuated", "turned_v", "values", "scores", "scores_read", "masked", "max", "exp",
                 "added", "summed", "probs", "probs_turned", "probsT", "mixed", "mix_hi", "mix_lo", "dve_rden")
        s_at = [{n: sem(f"{n}{l}") for n in names} for l in range(2)]
        s_mp, s_me, s_mvt, s_mv = map(sem, ("mem_projected", "mem_evacuated", "mem_turned", "mem_values"))
        s_fs, s_fh, s_fhi, s_fa = map(sem, ("ffn_silu", "ffn_hidden", "ffn_hidden_hi", "ffn_hidden_lo"))
        s_wi, s_qie, s_wie = map(sem, ("idx_weights", "idx_qk_sb", "idx_weights_sb"))
        s_cch, s_ctr, s_chi, s_clo, s_isc, s_rl, s_acc, s_sel, s_tk = map(
            sem, ("latent_chain", "latent_turned", "latent_hi", "latent_lo", "idx_scores", "idx_relu", "idx_added",
                  "keys_chosen", "topk_chain"))
        s_lg, s_ex2, s_rch, s_sl, s_rank, s_tab = map(
            sem, ("logits", "gate_exp", "route_chain", "chosen", "ranked", "passes_known"))
        s_ring = [sem(f"ring_in{s}") for s in range(RING)]
        s_S, s_SG, s_gat, s_ghi, s_glo, s_sgt, s_sgte = map(
            sem, ("pick_ready", "put_ready", "gathered", "tokens_hi", "tokens_lo", "put_turned", "putT"))
        s_silu, s_h, s_ht, s_ehi, s_elo, s_y, s_cmb, s_xadd = map(
            sem, ("silu_done", "hidden", "hidden_turned", "hidden_hi", "hidden_lo", "y_out", "combined", "x_added"))
        s_fin, s_out, s_fgin = map(sem, ("final", "stored", "final_gain_in"))

        NORM_MEM, NORM_MIX0, NORM_FFN0, NORM_MIX1, NORM_FFN1, NORM_END = range(6)
        GCOL = (G_MEM, G_MIX0, G_FFN0, G_MIX1, G_FFN1)
        XR = {NORM_MIX0: 0, NORM_FFN0: 2, NORM_MIX1: 4, NORM_FFN1: 6}

        def views(pair):
            n0 = SEQ if pair.cross else P
            w = n0 + SEQ
            return (z[:, 0:pair.nbr * w].rearrange("p (b s) -> p b s", b=pair.nbr),
                    pr[:, 0:pair.nbr * w].rearrange("p (b s) -> p b s", b=pair.nbr), n0)

        def width(pair, m):
            return RC * P if pair.kind == "odd" and m > 0 else UNIT

        def ring_slot(i):
            return (i + 3) % RING

        block = ctx.enter_context(nc.Block())

        @block.sync
        def _(sp):
            def load(i, first, units, src, n=UNIT):
                prev = [U.previous[u] for u in units]
                if prev[0] is not None:
                    sp.wait_ge(s_lo, along(i, first, [p + 1 for p in prev]))
                slot = U.slot[units[0]]
                dst = raw[slot][:, 0:n].rearrange("p (c n) -> p c n", c=src.shape[1])
                sp.dma_start(dst, src).then_inc(s_raw[slot], 16)

            def mat(pair, m):
                l, g = pair.l, pair.g
                if pair.cross:
                    col = (Q_X, O_X)[l] + (g - PAIRS) * P
                    return w_in[l][:, :, col:col + P]
                if l == 0:
                    return w_in[0][:, :, bass.ds(m * D + g * P, P)]
                return (w_in[1], w_uk, w_uv)[m][:, :, bass.ds(g * P, P)]

            def load_pair(pair):
                for m in range(pair.mats):
                    load(pair.idx, pair.span[0], pair.unit(m), mat(pair, m), width(pair, m))

            def stream_loads(l):
                span = range(1, PAIRS // 2)
                load_pair(pair_at(l, 0))
                load_pair(pair_at(l, 1))
                with sp.Fori(1, PAIRS // 2) as i:
                    for par in range(2):
                        load_pair(Pair(l, i, par, span))
                for g in range(PAIRS, NPAIR):
                    load_pair(pair_at(l, g))
                for ch in range(NPAIR):
                    load(0, 0, [U.at[("out", l, ch)]], w_o[l][:, ch:ch + 1, :])

            sp.dma_start(XH[:, :, :], mem_d).then_inc(s_mem, 16)
            sp.dma_start(con[:, :], consts).then_inc(s_con, 16)
            sp.dma_start(relb[:, :], rel_bias).then_inc(s_rel, 16)
            sp.dma_start(gn[:, :], gains).then_inc(s_con, 16)
            sp.dma_start(X[:, :, :], x_d).then_inc(s_x, 16)
            for n in range(8):
                l, q = n // 4, n % 4
                load(0, 0, [U.at[("mem", n)]], w_kv[l][:, :, q * P:(q + 1) * P])
            sp.dma_start(wwi, w_in[1][:, :, O_WI:O_WI + IDX_HEADS]).then_inc(s_ww, 16)
            stream_loads(0)

            def ffn_load(i, first, ns):
                kind, c0 = FFN[ns[0]]
                c = along(i, first, [FFN[n][1] for n in ns])
                src = ffn_w[kind][:, bass.ds(c, 1), :] if kind == "down" else ffn_w[kind][:, :, bass.ds(c * P, P)]
                load(i, first, [U.at[("ffn", n)] for n in ns], src)

            for n in range(8):
                ffn_load(0, 0, [n])
            span = range(1, FFN_LOOPS)
            with sp.Fori(1, FFN_LOOPS) as i:
                for k in range(6):
                    ffn_load(i, 1, [2 + 6 * b + k for b in span])
            for n in range(2 + 6 * FFN_LOOPS, len(FFN)):
                ffn_load(0, 0, [n])

            for n in range(2):
                load(0, 0, [U.at[("idx", n)]], w_in[1][:, 4 * n:4 * n + 4, O_C:O_C + RANK])
            for n in range(4):
                load(0, 0, [U.at[("idx", 2 + n)]], w_in[1][:, :, O_QI + n * P:O_QI + (n + 1) * P])
            u = U.at[("idx", 6)]
            sp.wait_ge(s_lo, U.previous[u] + 1)
            for half in range(2):
                dst = raw[U.slot[u]].rearrange("p (c n) -> p c n", c=DC)[:, :, half * HD:(half + 1) * HD]
                sp.dma_start(dst, w_in[1][:, :, O_KI:O_KI + HD]).then_inc(s_raw[U.slot[u]], 16)
            stream_loads(1)

            def half_load(i, e):
                (kind, j), h = ORDER[i // 2], i % 2
                if kind == "down":
                    src = expert_w[kind][:, bass.ds(e * (FE // P) + 4 * j + 2 * h, 2), :]
                else:
                    src = expert_w[kind][:, bass.ds(e * DC + 4 * h, 4), j * FT:(j + 1) * FT]
                s = ring_slot(i)
                dst = ring[s].rearrange("p (c n) -> p c n", c=src.shape[1])
                sp.dma_start(dst, src).then_inc(s_ring[s], 16)

            def half_free(i, before):
                sp.wait_ge(s_lo, before + 2 * (i - RING) + 2)

            sp.wait_ge(s_at[1]["scores_read"], 2 * PAIRS + 1)
            sp.dma_start(wr, w_router).then_inc(s_wr, 16)
            for i in range(4):
                half_load(i, 0)
            sp.wait_ge(s_lo, BASE)
            for i in range(4, RING):
                half_load(i, 0)
            for i in range(RING, 2 * TILES):
                half_free(i, BASE)
                half_load(i, 0)
            sp.wait_ge(s_isc, IDX_HEADS)
            sp.dma_start(fin_gain, bass.AP(final_norm.tensor, 0, [[0, P], [1, D]])).then_inc(s_fgin, 16)
            with sp.Fori(1, EXPERTS) as p:
                for i in range(2 * TILES):
                    half_free(i, PASS_UNITS * p + BASE)
                    half_load(i, p)
            sp.wait_ge(s_tab, 1)
            n_pass = sp.value_load(itab[0:1, 0:1], min_val=EXPERTS, max_val=NPASS)
            for k in range(EXTRA):
                e = sp.value_load(itab[0:1, 1 + k:2 + k], min_val=0, max_val=EXPERTS - 1)
                with sp.If(n_pass > EXPERTS + k):
                    for i in range(2 * TILES):
                        half_free(i, PASS_UNITS * (EXPERTS + k) + BASE)
                        half_load(i, e)
            sp.wait_ge(s_fin, TT)
            sp.dma_start(out_d, XH[:, :, :]).then_inc(s_out, 16)
            sp.wait_ge(s_out, 16)

        @block.gpsimd
        def _(pool):
            pool.wait_ge(s_eb, 1)
            src = ebuf.rearrange("h (o j) -> h o j", o=1).broadcast_to([HEADS, P, 384])
            pool.dma_start(scratch.rearrange("p h j -> h p j"), src).then_inc(s_scrw, 16)
            pool.wait_ge(s_scrw, 16)
            skew = bass.AP(scratch.tensor, P - 1, [[HEADS * 384 - 1, P], [384, HEADS], [1, 256]])
            pool.dma_start(bias, skew).then_inc(s_bias, 16)
            pool.wait_ge(s_bias, 16)
            pool.wait_ge(s_con, 32)

            def mask_pair(g, par, first):
                if not first:
                    pool.wait_ge(s_at[0]["scores_read"], 2 * g - 1)
                for b in range(NBR):
                    m = con[:, C_MASK + b * 256:C_MASK + (b + 1) * 256].rearrange("p (o s) -> p o s", o=1)
                    nc.gpsimd.tensor_tensor(bmp[:, par, :, b, :], bias[:, bass.ds(2 * g, 2), :],
                                            m.broadcast_to([P, 2, 256]), ALU.add).then_inc(s_bm, 1)

            mask_pair(0, 0, True)
            mask_pair(1, 1, True)
            with pool.Fori(1, PAIRS // 2) as i:
                for par in range(2):
                    mask_pair(2 * i + par, par, False)

        @block.tensor
        def _(pe):
            mm, tr = nc.tensor.matmul, nc.tensor.transpose

            def mm3(dst, a, b, start, stop, **kw):
                mm(dst, a[0], b[0], start=start, stop=False, **kw)
                mm(dst, a[0], b[1], start=False, stop=False, **kw)
                return mm(dst, a[1], b[0], start=False, stop=stop, **kw)

            def split(i, first, units, c, n=UNIT):
                pe.wait_ge(s_lo, along(i, first, [u + 1 for u in units]))
                slot = U.slot[units[0]]
                return tuple(w[:, slot, 0:n].rearrange("p (c n) -> p c n", c=c) for w in (w_hi, w_lo))

            def part(pr_, *ix):
                return tuple(a[ix] for a in pr_)

            A_ = slice(None)
            HS, MS, CS = (h_hi, h_lo), (m_hi, m_lo), (c_hi, c_lo)

            def tok(t):
                return slice(t * P, (t + 1) * P)

            def norm_turn(k):
                pe.wait_ge(s_xh, TT * (k + 1))
                for c in range(DC):
                    if DC * k + c >= 4:
                        pe.wait_ge(s_nlo, DC * k + c - 3)
                    for t in range(TT):
                        last = tr(ps[:, 4 + c % 4, tok(t)], XH[:, t, c * P:(c + 1) * P], ident)
                    last.then_inc(s_ntr, 1)

            def norm_ready(k):
                pe.wait_ge(s_nlo, DC * (k + 1))

            def project(pair, m):
                S = s_at[pair.l]
                n = pair.before() + m
                if not (isinstance(n, int) and n < 2):
                    pe.wait_ge(S["evacuated"], n - 1)
                src, kc = (CS, RC) if pair.kind == "odd" and m > 0 else (HS, DC)
                w = split(pair.idx, pair.span[0], pair.unit(m), kc, width(pair, m))
                for c in range(kc):
                    last = mm3(ps[:, pair.bank(m), 0:SEQ], part(w, A_, c, A_), part(src, A_, c, A_), c == 0, c == kc - 1)
                last.then_inc(s_used, 1)

            def turn_values(pair):
                S = s_at[pair.l]
                pe.wait_ge(S["evacuated"], pair.before() + pair.mats)
                for t in range(TT):
                    last = tr(ps[:, 7, tok(t)], vT[:, tok(t)], ident)
                last.then_inc(S["turned_v"], 1)

            def keys(pair):
                return kx[:, pair.l * XPAIRS + pair.gs[0] - PAIRS, :] if pair.cross else kT[:, pair.par, :]

            def scores(pair, hh):
                S = s_at[pair.l]
                pe.wait_ge(S["evacuated"], pair.before() + (1 if pair.cross else pair.nbr + 1))
                pe.wait_ge(S["scores_read"], 2 * pair.g + hh + 1)
                r = slice(HD * hh, HD * hh + HD)
                k = keys(pair)
                for b in range(pair.nbr):
                    n0 = SEQ if pair.cross else P
                    mm(ps[:, 0, b * P:b * P + n0], qT[r, pair.par, b, 0:P], k[r, 0:n0], start=True, stop=True)
                    o = ps[:, 1 + b // 2, (b % 2) * 256:(b % 2) * 256 + 256]
                    last = mm(o, qT[r, pair.par, b, P:SEQ], k[r, :], start=True, stop=True)
                last.then_inc(S["scores"], 1)

            def turn_probs(pair, hh):
                S = s_at[pair.l]
                pe.wait_ge(S["probs"], 2 * pair.g + hh + 1)
                pe.wait_ge(S["probsT"], 2 * pair.g + hh + 1)
                for a, b in ([(0, 0), (1, 2), (2, 1), (3, 3)] if pair.cross else [(0, 0), (1, 1), (2, 2)]):
                    last = tr(ps[:, 5, tok(b)], pn[:, tok(a)], ident)
                last.then_inc(S["probs_turned"], 1)

            def mix(pair, hh):
                S = s_at[pair.l]
                pe.wait_ge(S["probsT"], 2 * pair.g + hh + 2)
                if hh == 0:
                    pe.wait_ge(S["mix_lo"], pair.g + 1)
                    if not pair.cross:
                        pe.wait_ge(S["values"], pair.g + 1)
                o = ps[HD * hh:HD * hh + HD, 6, :]
                v = (vx[:, pair.l * XPAIRS + pair.gs[0] - PAIRS, :, :] if pair.cross else vN[:, :, :])
                v = v[:, :, HD * hh:HD * hh + HD]
                mm(o[:, 0:SEQ], v[:, 0, :], pts[:, 0:SEQ], start=True, stop=False)
                if pair.cross:
                    last = mm(o[:, 0:SEQ], v[:, 1, :], pts[:, SEQ:2 * SEQ], start=False, stop=True)
                else:
                    last = mm(o[:, P:SEQ], v[:, 1, :], pts[:, SEQ:SEQ + P], start=False, stop=True)
                last.then_inc(S["mixed"], 1)

            def step(now, nxt, aft):
                def p(m):
                    if nxt is not None and m < nxt.mats:
                        project(nxt, m)
                scores(now, 0)
                if not now.cross:
                    turn_values(now)
                p(0)
                scores(now, 1)
                p(1)
                turn_probs(now, 0)
                p(2)
                mix(now, 0)
                p(3)
                turn_probs(now, 1)
                p(4)
                mix(now, 1)

            def stream(l):
                pe.sem_inc(s_at[l]["mixed"], 1)
                pe.sem_inc(s_at[l]["probs_turned"], 1)
                first = pair_at(l, 0)
                for m in range(first.mats):
                    project(first, m)
                steps(l, pe, step)

            def out_project(l):
                S = s_at[l]
                pe.wait_ge(S["scores_read"], 2 * NPAIR + 1)
                pe.wait_ge(S["evacuated"], pair_at(l, NPAIR - 1).before() + 1)
                for ch in range(NPAIR):
                    pe.wait_ge(S["mix_lo"], ch + 2)
                    w = split(0, 0, [U.at[("out", l, ch)]], 1)
                    for t in range(TT):
                        for hf in range(2):
                            last = mm3(ps[:, 2 * t + hf, :], part(MS, A_, ch, tok(t)),
                                       part(w, A_, 0, slice(hf * 512, (hf + 1) * 512)), ch == 0, ch == NPAIR - 1)
                    last.then_inc(s_used, 1)

            pe.wait_ge(s_con, 32)
            pe.wait_ge(s_rel, 16)
            mm(ps[0:HEADS, 0, 0:384], relb[:, :], con[0:BUCKETS, C_HOT:C_HOT + 384], start=True, stop=True).then_inc(s_e, 1)
            norm_turn(NORM_MEM)
            norm_ready(NORM_MEM)
            for n in range(8):
                w = split(0, 0, [U.at[("mem", n)]], DC)
                if n >= 2:
                    pe.wait_ge(s_me, n - 1)
                for c in range(DC):
                    last = mm3(ps[:, 1 + n % 2, 0:SEQ], part(w, A_, c, A_), part(MS, A_, c, A_), c == 0, c == DC - 1)
                last.then_inc(s_used, 1)
                if n % 4 >= 2:
                    pe.wait_ge(s_me, n + 1)
                    v = 2 * (n // 4) + n % 2
                    if v:
                        pe.wait_ge(s_mv, v)
                    for t in range(TT):
                        last = tr(ps[:, 3, tok(t)], vT[:, tok(t)], ident)
                    last.then_inc(s_mvt, 1)
            norm_turn(NORM_MIX0)
            norm_ready(NORM_MIX0)
            pe.wait_ge(s_eb, 1)
            pe.wait_ge(s_mv, 4)
            stream(0)
            out_project(0)
            norm_turn(NORM_FFN0)
            norm_ready(NORM_FFN0)

            def ffn_unit(i, first, ns, start=False, stop=False):
                kind, c0 = FFN[ns[0]]
                c = along(i, first, [FFN[n][1] for n in ns])
                w = split(i, first, [U.at[("ffn", n)] for n in ns], 1 if kind == "down" else DC)
                par = c0 % 2
                if kind == "down":
                    pe.wait_ge(s_fa, c + 1)
                    for t in range(TT):
                        for hf in range(2):
                            last = mm3(ps[:, 2 * t + hf, :], part((f_hi, f_lo), A_, par, tok(t)),
                                       part(w, A_, 0, slice(hf * 512, (hf + 1) * 512)), start, stop, skip_group_check=True)
                    last.then_inc(s_used, 1)
                    return
                if c0 >= 2:
                    pe.wait_ge(s_fh, c - 1)
                for k in range(DC):
                    last = mm3(ps[:, (4 if kind == "gate" else 6) + par, 0:SEQ], part(w, A_, k, A_), part(HS, A_, k, A_),
                               k == 0, k == DC - 1)
                last.then_inc(s_used, 1)

            ffn_unit(0, 0, [0])
            ffn_unit(0, 0, [1])
            pe.wait_ge(s_xr, XR[NORM_FFN0])
            for n in range(2, 8):
                ffn_unit(0, 0, [n], start=FFN[n] == ("down", 0))
            span = range(1, FFN_LOOPS)
            with pe.Fori(1, FFN_LOOPS) as i:
                for k in range(6):
                    ffn_unit(i, 1, [2 + 6 * b + k for b in span])
            for n in range(2 + 6 * FFN_LOOPS, len(FFN)):
                ffn_unit(0, 0, [n], stop=FFN[n] == ("down", FC - 1))

            norm_turn(NORM_MIX1)
            norm_ready(NORM_MIX1)
            pe.wait_ge(s_xr, XR[NORM_MIX1])
            for n in range(2):
                w = split(0, 0, [U.at[("idx", n)]], 4)
                for t in range(TT):
                    for c in range(4):
                        last = mm3(ps[:, t, 0:RANK], part(HS, A_, 4 * n + c, tok(t)), part(w, A_, c, A_),
                                   n == 0 and c == 0, n == 1 and c == 3, skip_group_check=True)
                last.then_inc(s_used, 1)

            def narrow(bank, w):
                for t in range(TT):
                    for a in range(2):
                        for c in range(DC):
                            last = mm(ps[:, bank, t * 8:(t + 1) * 8], HS[a][:, c, tok(t)].bitcast(F32), w[:, c, :],
                                      start=(a == 0 and c == 0), stop=(a == 1 and c == DC - 1))
                return last
            pe.wait_ge(s_ww, 16)
            narrow(2, wwi).then_inc(s_wi, 1)
            for j in range(5):
                w = split(0, 0, [U.at[("idx", 2 + j)]], DC)
                for c in range(DC):
                    last = mm3(ps[:, 3 + j // 2, (j % 2) * SEQ:(j % 2 + 1) * SEQ], part(w, A_, c, A_), part(HS, A_, c, A_),
                               c == 0, c == DC - 1)
                last.then_inc(s_used, 1)
            pe.wait_ge(s_cch, 4)
            for c in range(RC):
                for t in range(TT):
                    last = tr(ps[:, 6, c * SEQ + t * P:c * SEQ + (t + 1) * P], cN[:, t, c * P:(c + 1) * P], ident)
            last.then_inc(s_ctr, 1)
            pe.wait_ge(s_qie, 1)
            for h in range(IDX_HEADS):
                if h >= 2:
                    pe.wait_ge(s_rl, h - 1)
                r = slice(HD * (h % 2), HD * (h % 2) + HD)
                mm(ps[:, h % 2, 0:P], qiT[r, h // 2, 0:P], kiT[r, 0:P], start=True, stop=True)
                mm(ps[:, h % 2, P:CAUSAL], qiT[r, h // 2, P:SEQ], kiT[r, :], start=True, stop=True).then_inc(s_isc, 1)
            pe.wait_ge(s_clo, RC)
            pe.wait_ge(s_rl, IDX_HEADS)
            stream(1)
            out_project(1)
            norm_turn(NORM_FFN1)
            norm_ready(NORM_FFN1)
            pe.wait_ge(s_wr, 16)
            narrow(7, wr).then_inc(s_lg, 1)
            pe.wait_ge(s_sl, 1)
            mm(ps[:, 6, 0:8], tri, sel[:, 0, :], start=True, stop=True)
            mm(ps[:, 6, 8:16], ones, sel[:, 0, :], start=True, stop=False)
            mm(ps[:, 6, 8:16], tri, sel[:, 1, :], start=False, stop=True)
            mm(ps[:, 6, 16:24], ones, sel[:, 0, :], start=True, stop=False)
            mm(ps[:, 6, 16:24], ones, sel[:, 1, :], start=False, stop=True).then_inc(s_rank, 1)
            pe.wait_ge(s_tab, 1)
            n_pass = pe.value_load(itab[0:1, 0:1], min_val=EXPERTS, max_val=NPASS)

            def gather(p):
                pe.wait_ge(s_S, p + 1)
                for c in range(DC):
                    for t in range(TT):
                        last = mm(ps[:, 5 + c // 4, (c % 4) * P:(c % 4 + 1) * P], XH[:, t, c * P:(c + 1) * P], Sg[:, t, :],
                                  start=(t == 0), stop=(t == TT - 1))
                last.then_inc(s_gat, 1)

            def combine(p):
                pe.wait_ge(s_sgte, p + 1)
                pe.wait_ge(s_y, p + 1)
                for t in range(TT):
                    for hf in range(2):
                        last = mm(ps[:, (5, 2)[t] + hf, :], SGT[:, tok(t)], ysb[:, hf * 512:(hf + 1) * 512],
                                  start=True, stop=True)
                    last.then_inc(s_cmb, 1)

            def expert_unit(u, p):
                (kind, j), q = ORDER[u // 4], u % 4
                pe.wait_ge(s_lo, PASS_UNITS * p + BASE + u + 1)
                slot = u % SLOTS
                c = 1 if kind == "down" else 2
                w = tuple(a[:, slot, :].rearrange("p (c n) -> p c n", c=c) for a in (w_hi, w_lo))
                if kind == "down":
                    if q == 0:
                        pe.wait_ge(s_elo, NT * p + j + 2)
                    for hf in range(2):
                        last = mm3(ps[:, 2 + hf, :], part((e_hi, e_lo), A_, q, A_),
                                   part(w, A_, 0, slice(hf * 512, (hf + 1) * 512)), j == 0 and q == 0, j == NT - 1 and q == 3)
                else:
                    if q == 0:
                        pe.wait_ge(s_silu if kind == "gate" else s_h, NT * p + j + 1)
                    for k in range(2):
                        last = mm3(ps[:, 0 if kind == "gate" else 1, :], part((g_hi, g_lo), A_, 2 * q + k, A_),
                                   part(w, A_, k, A_), q == 0 and k == 0, q == 3 and k == 1)
                last.then_inc(s_used, 1)

            def turn_hidden(j, p):
                pe.wait_ge(s_h, NT * p + j + 2)
                pe.wait_ge(s_elo, NT * p + j + 1)
                for k in range(4):
                    last = tr(ps[:, 4, tok(k)], eh[:, tok(k)], ident)
                last.then_inc(s_ht, 1)

            gather(0)
            with pe.Fori(0, n_pass) as p:
                pe.wait_ge(s_glo, p + 1)
                for u in range(PASS_UNITS):
                    kind, j = ORDER[u // 4]
                    if u % 4 == 0:
                        if kind == "up" and j:
                            turn_hidden(j - 1, p)
                        if kind == "gate" and j == 1:
                            combine(p)
                        if kind == "down" and j == 0:
                            pe.wait_ge(s_xadd, TT * p + 3)
                        if kind == "down" and j == NT - 1:
                            gather(p + 1)
                            pe.wait_ge(s_SG, p + 1)
                            for t in range(TT):
                                last = tr(ps[:, 7, tok(t)], SG[:, t, :], ident)
                            last.then_inc(s_sgt, 1)
                            turn_hidden(NT - 1, p)
                    expert_unit(u, p)
            combine(n_pass)

        @block.scalar
        def _(act):
            A = nc.scalar.activation

            def hi(i, first, units, n=UNIT):
                slot = U.slot[units[0]]
                act.wait_ge(s_raw[slot], along(i, first, [16 * U.loads[u] for u in units]))
                prev = [U.previous[u] for u in units]
                if prev[0] is not None:
                    act.wait_ge(s_used, along(i, first, [p + 1 for p in prev]))
                nc.scalar.copy(w_hi[:, slot, 0:n], raw[slot][:, 0:n]).then_inc(s_hi, 1)

            def hi_mat(pair, m):
                if pair is not None and m < pair.mats:
                    hi(pair.idx, pair.span[0], pair.unit(m), width(pair, m))

            def norm_stats(k):
                src = XH if k == NORM_MEM else X
                if k == NORM_MEM:
                    act.wait_ge(s_mem, 16)
                elif k == NORM_MIX0:
                    act.wait_ge(s_x, 16)
                    act.wait_ge(s_rstd, 1)
                elif k == NORM_END:
                    act.wait_ge(s_xadd, TT * n_pass_[0] + 3)
                else:
                    act.wait_ge(s_xr, XR[k])
                for t in range(TT):
                    last = A((z, pr)[t][:, 0:D], src[:, t, :], ACT.Square, accum_out=ss[:, t:t + 1])
                last.then_inc(s_ss, 1)
                act.wait_ge(s_ms, k + 1)
                A(sd, ms, ACT.Sqrt).then_inc(s_sd, 1)

            def norm_hi(k):
                act.wait_ge(s_con, 32)
                dst = m_hi if k == NORM_MEM else h_hi
                for c in range(DC):
                    act.wait_ge(s_ntr, DC * k + c + 1)
                    A(dst[:, c, :], ps[:, 4 + c % 4, 0:SEQ], ACT.Copy,
                      scale=gn[:, GCOL[k] + c:GCOL[k] + c + 1]).then_inc(s_nhi, 1)

            def evac(pair, m):
                S = s_at[pair.l]
                if pair is None or m >= pair.mats:
                    return
                act.wait_ge(s_used, along(pair.idx, pair.span[0], [u + 1 for u in pair.unit(m)]))
                if not (isinstance(pair.g, int) and pair.g < 2):
                    act.wait_ge(S["mixed"], 2 * pair.g - 1)
                if not pair.cross and m == pair.nbr + 1 and not (isinstance(pair.g, int) and pair.g < 1):
                    act.wait_ge(S["turned_v"], pair.g)
                dst = qT[:, pair.par, m, :] if m < pair.nbr else kT[:, pair.par, :] if m == pair.nbr else vT[:, :]
                nc.scalar.copy(dst, ps[:, pair.bank(m), 0:SEQ]).then_inc(S["evacuated"], 1)

            def exps(pair, hh):
                S = s_at[pair.l]
                act.wait_ge(S["max"], 2 * pair.g + hh + 1)
                zv, pv, n0 = views(pair)
                for t, (a, b) in enumerate(((0, n0), (n0, n0 + SEQ))):
                    last = A(pv[:, :, a:b], zv[:, :, a:b], ACT.Exp, bias=nmx[:, t:t + 1], accum_out=den[:, t:t + 1])
                last.then_inc(S["exp"], 1)

            def probsT(pair, hh):
                S = s_at[pair.l]
                act.wait_ge(S["probs_turned"], 2 * pair.g + hh + 2)
                act.wait_ge(S["mixed"], 2 * pair.g + hh + 1)
                n = 512 if pair.cross else CAUSAL
                nc.scalar.copy(pts[:, 0:n], ps[:, 5, 0:n]).then_inc(S["probsT"], 1)

            def step(now, nxt, aft):
                S = s_at[now.l]

                def e(m):
                    if nxt is not None and m < nxt.mats:
                        evac(nxt, m)
                if not now.cross:
                    act.wait_ge(S["turned_v"], now.g + 1)
                    nc.scalar.copy(vN[:, :, :].rearrange("p t n -> p (t n)"), ps[:, 7, 0:SEQ]).then_inc(S["values"], 1)
                exps(now, 0)
                e(0)
                hi_mat(aft, 0)
                exps(now, 1)
                e(1)
                hi_mat(aft, 1)
                probsT(now, 0)
                e(2)
                hi_mat(aft, 2)
                e(3)
                hi_mat(aft, 3)
                probsT(now, 1)
                e(4)
                hi_mat(aft, 4)
                act.wait_ge(S["mixed"], 2 * now.g + 3)
                nc.scalar.copy(m_hi[:, bass.ds(now.g, 1), :].rearrange("p o n -> p (o n)"), ps[:, 6, 0:SEQ]).then_inc(S["mix_hi"], 1)
                if aft is None and nxt is not None:
                    for ch in range(5):
                        hi(0, 0, [U.at[("out", now.l, ch)]])

            def stream(l):
                act.sem_inc(s_at[l]["probsT"], 1)
                a, b = pair_at(l, 0), pair_at(l, 1)
                for m in range(a.mats):
                    hi_mat(a, m)
                for m in range(a.mats):
                    evac(a, m)
                    hi_mat(b, m)
                steps(l, act, step)
                for ch in range(5, NPAIR):
                    hi(0, 0, [U.at[("out", l, ch)]])

            norm_stats(NORM_MEM)
            act.wait_ge(s_e, 1)
            nc.scalar.copy(ebuf, ps[0:HEADS, 0, 0:384]).then_inc(s_eb, 1)
            norm_hi(NORM_MEM)
            for n in range(SLOTS):
                hi(0, 0, [U.at[("mem", n)]])
            norm_stats(NORM_MIX0)
            for n in range(8):
                act.wait_ge(s_used, U.at[("mem", n)] + 1)
                q = 2 * (n // 4) + n % 2
                if n % 4 < 2:
                    nc.scalar.copy(kx[:, q, :], ps[:, 1 + n % 2, 0:SEQ]).then_inc(s_me, 1)
                else:
                    if q:
                        act.wait_ge(s_mvt, q)
                    nc.scalar.copy(vT[:, :], ps[:, 1 + n % 2, 0:SEQ]).then_inc(s_me, 1)
                    act.wait_ge(s_mvt, q + 1)
                    nc.scalar.copy(vx[:, q, :, :].rearrange("p t n -> p (t n)"), ps[:, 3, 0:SEQ]).then_inc(s_mv, 1)
                if n + SLOTS < 8:
                    hi(0, 0, [U.at[("mem", n + SLOTS)]])
            norm_hi(NORM_MIX0)
            act.wait_ge(s_scrw, 16)
            stream(0)
            norm_stats(NORM_FFN0)
            for n in range(SLOTS):
                hi(0, 0, [U.at[("ffn", n)]])
            norm_hi(NORM_FFN0)

            def silu(i, first, ns):
                if FFN[ns[0]][0] != "gate":
                    return
                c0 = FFN[ns[0]][1]
                c = along(i, first, [FFN[n][1] for n in ns])
                act.wait_ge(s_used, along(i, first, [U.at[("ffn", n)] + 1 for n in ns]))
                if c0 >= 2:
                    act.wait_ge(s_fh, c - 1)
                A(fsg[:, c0 % 2, :], ps[:, 4 + c0 % 2, 0:SEQ], ACT.Silu).then_inc(s_fs, 1)

            def after_unit(n):
                return U.at[("ffn", n)] + SLOTS

            for n in range(8):
                silu(0, 0, [n])
                hi(0, 0, [after_unit(n)])
            span = range(1, FFN_LOOPS - 1)
            with act.Fori(1, FFN_LOOPS - 1) as i:
                for k in range(6):
                    ns = [2 + 6 * b + k for b in span]
                    silu(i, 1, ns)
                    hi(i, 1, [after_unit(n) for n in ns])
            for n in range(2 + 6 * (FFN_LOOPS - 1), len(FFN)):
                silu(0, 0, [n])
                hi(0, 0, [after_unit(n)])
            norm_stats(NORM_MIX1)
            norm_hi(NORM_MIX1)
            hi(0, 0, [U.at[("idx", 6)]])
            act.wait_ge(s_used, U.at[("idx", 1)] + 1)
            for t in range(TT):
                last = A((tmp, pts)[t][:, 0:RANK], ps[:, t, 0:RANK], ACT.Square, accum_out=ss[:, t:t + 1])
            last.then_inc(s_cch, 1)
            act.wait_ge(s_cch, 2)
            A(sd, ms, ACT.Sqrt).then_inc(s_cch, 1)
            act.wait_ge(s_used, U.at[("idx", 6)] + 1)
            nc.scalar.copy(qiT[:, 0:2, :].rearrange("p a n -> p (a n)"), ps[:, 3, :])
            nc.scalar.copy(qiT[:, 2:4, :].rearrange("p a n -> p (a n)"), ps[:, 4, :])
            nc.scalar.copy(kiT[:, :], ps[:, 5, 0:SEQ]).then_inc(s_qie, 1)
            act.wait_ge(s_ctr, 1)
            for c in range(RC):
                A(c_hi[:, c, :], ps[:, 6, c * SEQ:(c + 1) * SEQ], ACT.Copy, scale=gn[:, G_KV + c:G_KV + c + 1]).then_inc(s_chi, 1)
            for h in range(IDX_HEADS):
                act.wait_ge(s_isc, h + 1)
                if h >= 2:
                    act.wait_ge(s_acc, h - 1)
                A(rl[:, h % 2, :], ps[:, h % 2, 0:CAUSAL], ACT.Relu, scale=HD ** -0.5).then_inc(s_rl, 1)
            stream(1)
            norm_stats(NORM_FFN1)
            norm_hi(NORM_FFN1)

            def expert_hi(u, p, before=None):
                i, slot = u // 2, u % SLOTS
                s = ring_slot(i)
                act.wait_ge(s_ring[s], 16 * (2 * TILES // RING * p + i // RING + 1))
                act.wait_ge(s_used, PASS_UNITS * p + BASE + u - SLOTS + 1)
                nc.scalar.copy(w_hi[:, slot, :], ring[s][:, (u % 2) * UNIT:(u % 2 + 1) * UNIT]).then_inc(s_hi, 1)

            act.wait_ge(s_rch, 1)
            A(ex2, dlt, ACT.Exp).then_inc(s_ex2, 1)
            act.wait_ge(s_tab, 1)
            n_pass = act.value_load(itab[0:1, 0:1], min_val=EXPERTS, max_val=NPASS)
            n_pass_ = [n_pass]
            act.sem_inc(s_silu, 1)

            def gathered(p):
                act.wait_ge(s_gat, p + 1)
                for c in range(DC):
                    last = A(g_hi[:, c, :], ps[:, 5 + c // 4, (c % 4) * P:(c % 4 + 1) * P], ACT.Copy,
                             scale=gn[:, G_FFN1 + c:G_FFN1 + c + 1])
                last.then_inc(s_ghi, 1)

            def hidden_hi(j, p):
                act.wait_ge(s_ht, NT * p + j + 1)
                nc.scalar.copy(e_hi.rearrange("p k n -> p (k n)"), ps[:, 4, :]).then_inc(s_ehi, 1)

            def y_out(need):
                act.wait_ge(s_used, need)
                nc.scalar.copy(ysb, ps[:, 2:4, :].rearrange("p k n -> p (k n)")).then_inc(s_y, 1)

            gathered(0)
            with act.Fori(0, n_pass) as p:
                for u in range(PASS_UNITS):
                    v = u - SLOTS
                    if u == 5:
                        y_out(PASS_UNITS * p + BASE)
                    if v >= 0 and v % 4 == 3:
                        kind, j = ORDER[v // 4]
                        if kind == "gate":
                            if j:
                                hidden_hi(j - 1, p)
                            act.wait_ge(s_used, PASS_UNITS * p + BASE + v + 1)
                            act.wait_ge(s_h, NT * p + j + 1)
                            A(esg, ps[:, 0, :], ACT.Silu).then_inc(s_silu, 1)
                    expert_hi(u, p)
                gathered(p + 1)
                act.wait_ge(s_sgt, p + 1)
                nc.scalar.copy(SGT, ps[:, 7, 0:256]).then_inc(s_sgte, 1)
                hidden_hi(NT - 1, p)
            y_out(PASS_UNITS * n_pass + BASE)
            norm_stats(NORM_END)

        @block.vector
        def _(dve):
            V = nc.vector

            def rest(dst, src, lead):
                return V.tensor_tensor(dst, src, lead.bitcast(F32), ALU.subtract)

            def lo(i, first, units, n=UNIT):
                slot = U.slot[units[0]]
                dve.wait_ge(s_hi, along(i, first, [u + 1 for u in units]))
                rest(w_lo[:, slot, 0:n], raw[slot][:, 0:n], w_hi[:, slot, 0:n]).then_inc(s_lo, 1)

            def lo_mat(pair, m):
                if pair is not None and m < pair.mats:
                    lo(pair.idx, pair.span[0], pair.unit(m), width(pair, m))

            def rest_scaled(dst, src, gain, lead):
                return V.scalar_tensor_tensor(out=dst, in0=src, scalar=gain, in1=lead.bitcast(F32),
                                              op0=ALU.mult, op1=ALU.subtract)

            def norm_rows(k):
                src = XH if k == NORM_MEM else X
                dve.wait_ge(s_ss, k + 1)
                V.tensor_scalar(ms, ss, 1.0 / D, EPS, ALU.mult, ALU.add).then_inc(s_ms, 1)
                dve.wait_ge(s_sd, k + 1)
                V.reciprocal(rstd, sd).then_inc(s_rstd, 1)
                dve.wait_ge(s_rstd, k + 1)
                if k == NORM_MIX0:
                    dve.wait_ge(s_ntr, DC)
                for t in range(TT):
                    V.tensor_scalar(XH[:, t, :], src[:, t, :], rstd[:, t:t + 1], None, ALU.mult).then_inc(s_xh, 1)

            def norm_lo(k):
                hi_, lo_ = (m_hi, m_lo) if k == NORM_MEM else (h_hi, h_lo)
                for c in range(DC):
                    dve.wait_ge(s_nhi, DC * k + c + 1)
                    rest_scaled(lo_[:, c, :], ps[:, 4 + c % 4, 0:SEQ], gn[:, GCOL[k] + c:GCOL[k] + c + 1],
                                hi_[:, c, :]).then_inc(s_nlo, 1)

            def head_scores(pair, hh):
                S = s_at[pair.l]
                n = 2 * pair.g + hh
                zv, pv, n0 = views(pair)
                dve.wait_ge(S["scores"], n + 1)
                if pair.kind == "even" and hh == 0:
                    dve.wait_ge(s_bm, NBR * pair.g + NBR)
                tiles = ((0, n0), (n0, n0 + SEQ))
                for t, (a, b) in enumerate(tiles):
                    src = ps[:, 0, 0:pair.nbr * (b - a)] if t == 0 else \
                        ps[:, 1:3, :].rearrange("p k n -> p (k n)")[:, 0:pair.nbr * SEQ]
                    src = src.rearrange("p (b s) -> p b s", b=pair.nbr)
                    if pair.cross:
                        last = V.tensor_scalar(zv[:, :, a:b], src, SCALE, None, ALU.mult)
                        continue
                    cols = slice(P, SEQ) if t == 0 else slice(0, SEQ)
                    add = bmp[:, pair.par, hh, :, cols] if pair.l == 0 else bias[:, bass.ds(n, 1), cols]
                    last = V.scalar_tensor_tensor(out=zv[:, :, a:b], in0=src, scalar=SCALE, in1=add,
                                                  op0=ALU.mult, op1=ALU.add)
                last.then_inc(S["scores_read"], 1)
                dve.wait_ge(S["scores_read"], n + 2)
                if pair.kind == "odd":
                    V.tensor_tensor(z[:, 0:CAUSAL], z[:, 0:CAUSAL], selm[:, :], ALU.add).then_inc(S["masked"], 1)
                    dve.wait_ge(S["masked"], n + 1)
                for t, (a, b) in enumerate(tiles):
                    last = V.tensor_reduce(nmx[:, t:t + 1], zv[:, :, a:b], mybir.AxisListType.XY, ALU.max, negate=True)
                last.then_inc(S["max"], 1)

            def head_probs(pair, hh):
                S = s_at[pair.l]
                n = 2 * pair.g + hh
                zv, pv, n0 = views(pair)
                dve.wait_ge(S["exp"], n + 1)
                V.reciprocal(rden, den).then_inc(S["dve_rden"], 1)
                src = pv[:, 0, :]
                if pair.nbr == NBR:
                    V.tensor_tensor(tmp[:, :], pv[:, 0, :], pv[:, 1, :], ALU.add).then_inc(S["added"], 1)
                    dve.wait_ge(S["added"], n + 1)
                    V.tensor_tensor(tmp[:, :], tmp[:, :], pv[:, 2, :], ALU.add).then_inc(S["summed"], 1)
                    dve.wait_ge(S["summed"], n + 1)
                    src = tmp[:, :]
                dve.wait_ge(S["dve_rden"], n + 1)
                dve.wait_ge(S["probs_turned"], n + 1)
                for t, (a, b) in enumerate(((0, n0), (n0, n0 + SEQ))):
                    last = V.tensor_scalar(pn[:, a:b], src[:, a:b], rden[:, t:t + 1], None, ALU.mult)
                last.then_inc(S["probs"], 1)

            def step(now, nxt, aft):
                S = s_at[now.l]
                head_scores(now, 0)
                lo_mat(aft, 0)
                head_probs(now, 0)
                head_scores(now, 1)
                lo_mat(aft, 1)
                head_probs(now, 1)
                lo_mat(aft, 2)
                lo_mat(aft, 3)
                lo_mat(aft, 4)
                dve.wait_ge(S["mix_hi"], now.g + 1)
                rest(m_lo[:, bass.ds(now.g, 1), :].rearrange("p o n -> p (o n)"), ps[:, 6, 0:SEQ],
                     m_hi[:, bass.ds(now.g, 1), :].rearrange("p o n -> p (o n)")).then_inc(S["mix_lo"], 1)
                if aft is None and nxt is not None:
                    for ch in range(5):
                        lo(0, 0, [U.at[("out", now.l, ch)]])

            def stream(l):
                dve.sem_inc(s_at[l]["scores_read"], 1)
                dve.sem_inc(s_at[l]["mix_lo"], 1)
                for g in range(2):
                    for m in range(pair_at(l, g).mats):
                        lo_mat(pair_at(l, g), m)
                if l == 1:
                    choose_keys()
                steps(l, dve, step)
                for ch in range(5, NPAIR):
                    lo(0, 0, [U.at[("out", l, ch)]])

            def residual(need):
                dve.wait_ge(s_used, need)
                for t in range(TT):
                    V.tensor_tensor(X[:, t, :], X[:, t, :], ps[:, 2 * t:2 * t + 2, :].rearrange("p k n -> p (k n)"),
                                    ALU.add).then_inc(s_xr, 1)

            norm_rows(NORM_MEM)
            norm_lo(NORM_MEM)
            for n in range(SLOTS):
                lo(0, 0, [U.at[("mem", n)]])
            norm_rows(NORM_MIX0)
            for n in range(SLOTS, 8):
                lo(0, 0, [U.at[("mem", n)]])
            norm_lo(NORM_MIX0)
            stream(0)
            residual(U.at[("out", 0, NPAIR - 1)] + 1)
            norm_rows(NORM_FFN0)
            for n in range(SLOTS):
                lo(0, 0, [U.at[("ffn", n)]])
            norm_lo(NORM_FFN0)

            def hidden(i, first, ns):
                if FFN[ns[0]][0] != "up":
                    return
                c0 = FFN[ns[0]][1]
                par = c0 % 2
                c = along(i, first, [FFN[n][1] for n in ns])
                dve.wait_ge(s_fs, c + 1)
                dve.wait_ge(s_used, along(i, first, [U.at[("ffn", n)] + 1 for n in ns]))
                V.tensor_tensor(fh[:, par, :], fsg[:, par, :], ps[:, 6 + par, 0:SEQ], ALU.mult).then_inc(s_fh, 1)
                dve.wait_ge(s_fh, c + 1)
                V.tensor_copy(f_hi[:, par, :], fh[:, par, :]).then_inc(s_fhi, 1)
                dve.wait_ge(s_fhi, c + 1)
                rest(f_lo[:, par, :], fh[:, par, :], f_hi[:, par, :]).then_inc(s_fa, 1)

            def after_unit(n):
                return U.at[("ffn", n)] + SLOTS

            for n in range(8):
                hidden(0, 0, [n])
                lo(0, 0, [after_unit(n)])
            span = range(1, FFN_LOOPS - 1)
            with dve.Fori(1, FFN_LOOPS - 1) as i:
                for k in range(6):
                    ns = [2 + 6 * b + k for b in span]
                    hidden(i, 1, ns)
                    lo(i, 1, [after_unit(n) for n in ns])
            for n in range(2 + 6 * (FFN_LOOPS - 1), len(FFN)):
                hidden(0, 0, [n])
                lo(0, 0, [after_unit(n)])
            residual(U.at[("ffn", len(FFN) - 1)] + 1)
            norm_rows(NORM_MIX1)
            norm_lo(NORM_MIX1)
            lo(0, 0, [U.at[("idx", 6)]])

            dve.wait_ge(s_cch, 1)
            V.tensor_scalar(ms, ss, 1.0 / RANK, EPS, ALU.mult, ALU.add).then_inc(s_cch, 1)
            dve.wait_ge(s_wi, 1)
            V.tensor_scalar(wis, ps[:, 2, 0:16].rearrange("p (t k) -> p t k", t=TT), IDX_HEADS ** -0.5, None,
                            ALU.mult).then_inc(s_wie, 1)
            dve.wait_ge(s_cch, 3)
            V.reciprocal(rstd, sd).then_inc(s_wie, 1)
            dve.wait_ge(s_wie, 2)
            for t in range(TT):
                last = V.tensor_scalar(cN[:, t, :], ps[:, t, 0:RANK], rstd[:, t:t + 1], None, ALU.mult)
            last.then_inc(s_cch, 1)
            dve.wait_ge(s_cch, 4)
            dve.wait_ge(s_chi, RC)
            for c in range(RC):
                rest_scaled(c_lo[:, c, :], ps[:, 6, c * SEQ:(c + 1) * SEQ], gn[:, G_KV + c:G_KV + c + 1],
                            c_hi[:, c, :]).then_inc(s_clo, 1)
            tiles = ((0, P), (P, CAUSAL))
            for h in range(IDX_HEADS):
                dve.wait_ge(s_rl, h + 1)
                if h:
                    dve.wait_ge(s_acc, h)
                for t, (a, b) in enumerate(tiles):
                    w = wis[:, t, h:h + 1]
                    if h == 0:
                        last = V.tensor_scalar(scr[:, 0, a:b], rl[:, 0, a:b], w, None, ALU.mult)
                    else:
                        last = V.scalar_tensor_tensor(out=scr[:, 0, a:b], in0=rl[:, h % 2, a:b], scalar=w,
                                                      in1=scr[:, 0, a:b], op0=ALU.mult, op1=ALU.add)
                last.then_inc(s_acc, 1)
            TOPK_STEPS = 2 * (TOPK // 8) + 1

            def choose_keys():
                tiles = ((0, P), (P, CAUSAL))
                dve.wait_ge(s_acc, IDX_HEADS)
                V.tensor_tensor(scr[:, 1, 0:P], scr[:, 0, 0:P], causal[:, P:SEQ], ALU.add)
                V.tensor_tensor(scr[:, 1, P:CAUSAL], scr[:, 0, P:CAUSAL], causal, ALU.add).then_inc(s_tk, 1)
                cur, n = 1, 1
                for _ in range(TOPK // 8):
                    dve.wait_ge(s_tk, n)
                    for t, (a, b) in enumerate(tiles):
                        last = V.max(ms8[:, t, :], scr[:, cur, a:b])
                    last.then_inc(s_tk, 1)
                    dve.wait_ge(s_tk, n + 1)
                    for t, (a, b) in enumerate(tiles):
                        last = V.match_replace(scr[:, 1 - cur, a:b], ms8[:, t, :], scr[:, cur, a:b], TAKEN)
                    last.then_inc(s_tk, 1)
                    cur, n = 1 - cur, n + 2
                dve.wait_ge(s_tk, n)
                V.tensor_scalar(scr[:, 1 - cur, :], scr[:, cur, :], -1e35, NEG, ALU.is_gt, ALU.mult).then_inc(s_tk, 1)
                dve.wait_ge(s_tk, n + 1)
                V.tensor_tensor(selm[:, 0:P], scr[:, 1 - cur, 0:P], causal[:, P:SEQ], ALU.add)
                V.tensor_tensor(selm[:, P:CAUSAL], scr[:, 1 - cur, P:CAUSAL], causal, ALU.add).then_inc(s_sel, 1)
                dve.wait_ge(s_sel, 1)
            stream(1)
            residual(U.at[("out", 1, NPAIR - 1)] + 1)
            norm_rows(NORM_FFN1)
            norm_lo(NORM_FFN1)

            chain = [0]

            def link(ins):
                chain[0] += 1
                ins.then_inc(s_rch, 1)
                dve.wait_ge(s_rch, chain[0])

            dve.wait_ge(s_lg, 1)
            V.tensor_copy(lg, ps[:, 7, 0:16].rearrange("p (t k) -> p t k", t=TT)).then_inc(s_tk, 1)
            n = TOPK_STEPS + 2
            dve.wait_ge(s_tk, n)
            for t in range(TT):
                last = V.max(top8[:, t, :], lg[:, t, :])
            last.then_inc(s_tk, 1)
            dve.wait_ge(s_tk, n + 1)
            link(V.tensor_tensor(dlt, top8[:, :, 1], top8[:, :, 0], ALU.subtract))
            for t in range(TT):
                last = V.max_index(uidx[:, t, :], top8[:, t, :], lg[:, t, :])
            link(last)
            link(V.tensor_copy(idxf, uidx[:, :, :]))
            for t in range(TT):
                V.tensor_scalar(oh0[:, t, :], iota8, idxf[:, t, 0:1], None, ALU.is_equal)
                last = V.tensor_scalar(oh1[:, t, :], iota8, idxf[:, t, 1:2], None, ALU.is_equal)
            link(last)
            V.tensor_tensor(sel, oh0, oh1, ALU.add).then_inc(s_sl, 1)
            dve.wait_ge(s_ex2, 1)
            link(V.tensor_scalar(den2, ex2, 1.0, None, ALU.add))
            link(V.reciprocal(g1, den2))
            link(V.tensor_tensor(g2, ex2, g1, ALU.mult))
            V.memset(slotc, -1.0)
            V.memset(gatec, 0.0)
            for t in range(TT):
                last = V.tensor_scalar(gate_e[:, t, :], oh0[:, t, :], g1[:, t:t + 1], None, ALU.mult)
            link(last)
            for t in range(TT):
                last = V.scalar_tensor_tensor(out=gatec[:, t, 0:EXPERTS], in0=oh1[:, t, :], scalar=g2[:, t:t + 1],
                                              in1=gate_e[:, t, :], op0=ALU.mult, op1=ALU.add)
            link(last)
            dve.wait_ge(s_rank, 1)
            rank = ps[:, 6, 0:16].rearrange("p (t k) -> p t k", t=TT)
            link(V.scalar_tensor_tensor(out=slot1, in0=rank, scalar=1.0, in1=sel, op0=ALU.add, op1=ALU.mult))
            V.tensor_scalar(slotc[:, :, 0:EXPERTS], slot1, 1.0, None, ALU.subtract)
            link(V.tensor_scalar(over, ps[:, 6, 16:24], CAP + 0.5, None, ALU.is_gt))
            src, dst = over, pa
            for sh, nxt in ((1, pb), (2, pc), (4, None)):
                V.tensor_copy(dst[:, 0:sh], src[:, 0:sh])
                link(V.tensor_tensor(dst[:, sh:8], src[:, sh:8], src[:, 0:8 - sh], ALU.add))
                src, dst = dst, nxt
            for k in range(EXTRA):
                last = V.scalar_tensor_tensor(out=ind[:, k, :], in0=src, scalar=k + 1.0, in1=over,
                                              op0=ALU.is_equal, op1=ALU.mult)
            link(last)
            link(V.tensor_scalar(tabf[:, 0:1], src[:, 7:8], float(EXPERTS), None, ALU.add))
            for k in range(EXTRA):
                link(V.scalar_tensor_tensor(out=junk8, in0=iota8, scalar=1.0, in1=ind[:, k, :], op0=ALU.mult,
                                            op1=ALU.mult, accum_out=tabf[:, 1 + k:2 + k]))
                for t in range(TT):
                    link(V.scalar_tensor_tensor(out=junk8, in0=slot1[:, t, :], scalar=4.0 * SEQ, in1=ind[:, k, :],
                                                op0=ALU.add, op1=ALU.mult,
                                                accum_out=slotc[:, t, EXPERTS + k:EXPERTS + k + 1]))
                    link(V.scalar_tensor_tensor(out=junk8, in0=gatec[:, t, 0:EXPERTS], scalar=1.0, in1=ind[:, k, :],
                                                op0=ALU.mult, op1=ALU.mult,
                                                accum_out=gatec[:, t, EXPERTS + k:EXPERTS + k + 1]))
            link(V.tensor_scalar(slotc[:, :, EXPERTS:NPASS], slotc[:, :, EXPERTS:NPASS], 4.0 * SEQ + 1 + CAP, None,
                                 ALU.subtract))
            V.tensor_copy(itab[:, :], tabf).then_inc(s_tab, 1)

            V.memset(SGT, 0.0).then_inc(s_sgte, 1)
            dve.sem_inc(s_h, 1)
            dve.sem_inc(s_elo, 1)
            dve.sem_inc(s_xadd, 1)

            def expert_lo(u, p):
                i, slot = u // 2, u % SLOTS
                dve.wait_ge(s_hi, PASS_UNITS * p + BASE + u + 1)
                rest(w_lo[:, slot, :], ring[ring_slot(i)][:, (u % 2) * UNIT:(u % 2 + 1) * UNIT], w_hi[:, slot, :]).then_inc(s_lo, 1)

            def pick(p):
                for t in range(TT):
                    last = V.tensor_scalar(Sg[:, t, :], iota, slotc[:, t, bass.ds(p, 1)], None, ALU.is_equal)
                last.then_inc(s_S, 1)

            def gathered(p):
                dve.wait_ge(s_ghi, p + 1)
                for c in range(DC):
                    last = rest_scaled(g_lo[:, c, :], ps[:, 5 + c // 4, (c % 4) * P:(c % 4 + 1) * P],
                                       gn[:, G_FFN1 + c:G_FFN1 + c + 1], g_hi[:, c, :])
                last.then_inc(s_glo, 1)

            def hidden_lo(j, p):
                dve.wait_ge(s_ehi, NT * p + j + 1)
                rest(e_lo.rearrange("p k n -> p (k n)"), ps[:, 4, :], e_hi.rearrange("p k n -> p (k n)")).then_inc(s_elo, 1)

            def add_rows(p):
                for t in range(TT):
                    dve.wait_ge(s_cmb, TT * p + t + 1)
                    b0 = (5, 2)[t]
                    V.tensor_tensor(X[:, t, :], X[:, t, :], ps[:, b0:b0 + 2, :].rearrange("p k n -> p (k n)"),
                                    ALU.add).then_inc(s_xadd, 1)

            pick(0)
            gathered(0)
            dve.wait_ge(s_tab, 1)
            n_pass = dve.value_load(itab[0:1, 0:1], min_val=EXPERTS, max_val=NPASS)
            with dve.Fori(0, n_pass) as p:
                for u in range(PASS_UNITS):
                    v = u - SLOTS
                    if v >= 0 and v % 4 == 3:
                        kind, j = ORDER[v // 4]
                        if kind == "gate" and j:
                            hidden_lo(j - 1, p)
                        if kind == "up":
                            dve.wait_ge(s_silu, NT * p + j + 2)
                            dve.wait_ge(s_used, PASS_UNITS * p + BASE + v + 1)
                            V.tensor_tensor(eh, esg, ps[:, 1, :], ALU.mult).then_inc(s_h, 1)
                            if j == 0:
                                dve.wait_ge(s_S, p + 1)
                                for t in range(TT):
                                    last = V.tensor_scalar(SG[:, t, :], Sg[:, t, :], gatec[:, t, bass.ds(p, 1)], None, ALU.mult)
                                last.then_inc(s_SG, 1)
                            if j == 1:
                                dve.wait_ge(s_SG, p + 1)
                                pick(p + 1)
                    if u == 15:
                        add_rows(p)
                    expert_lo(u, p)
                gathered(p + 1)
                hidden_lo(NT - 1, p)
            add_rows(n_pass)
            norm_rows(NORM_END)
            dve.wait_ge(s_xh, TT * (NORM_END + 1))
            dve.wait_ge(s_fgin, 16)
            for t in range(TT):
                V.tensor_tensor(XH[:, t, :], XH[:, t, :], fin_gain, ALU.mult).then_inc(s_fin, 1)


_INS = ["x", "mem", "rel_bias", "gains", "final_norm", "consts", "w_mem_kv", "w_out", "even_w_in", "even_w_gate",
        "even_w_up", "even_w_down", "odd_w_in", "odd_w_uk", "odd_w_uv", "odd_w_router", "odd_w_gate", "odd_w_up",
        "odd_w_down"]


def kernel(**inputs):
    import concourse.bacc as bacc
    from concourse.bass_utils import run_bass_kernel_spmd

    given = {k: np.ascontiguousarray(v) for k, v in inputs.items()}
    rows = [given["mem_norm"], given["mixer_norm"][0], given["ffn_norm"][0], given["mixer_norm"][1],
            given["ffn_norm"][1], given["odd_kv_norm"][0]]
    given["gains"] = np.ascontiguousarray(np.concatenate([r.reshape(-1, P) for r in rows]).T)
    given["consts"] = shape_constants()

    nc = bacc.Bacc("TRN2", target_bir_lowering=False, num_devices=1)
    arrays, args = {}, []
    for name in _INS:
        arrays[f"in_{name}"] = given[name]
        args.append(nc.dram_tensor(f"in_{name}", given[name].shape, mybir.dt.from_np(given[name].dtype),
                                   kind="ExternalInput").ap())
    args.append(nc.dram_tensor("out_0", (1, SEQ, D), F32, kind="ExternalOutput").ap())
    build(nc, *args)
    r = run_bass_kernel_spmd(nc, [arrays], core_ids=[0])
    return r.results[0]["out_0"]
```

```python
import math
from contextlib import ExitStack

import numpy as np

import concourse.bass as bass
from concourse import mybir

F32 = mybir.dt.float32
F32R = mybir.dt.float32r
I32 = mybir.dt.int32
U32 = mybir.dt.uint32
ALU = mybir.AluOpType
ACT = mybir.ActivationFunctionType

P = 128
D = 1024
DC = D // P
SEQ = 256
TT = SEQ // P
HEADS, HD = 16, 64
PAIRS = HEADS // 2
XPAIRS = 2
NPAIR = PAIRS + XPAIRS
SCALE = HD ** -0.5
EPS = 1e-6
NEG = -1e30
TAKEN = -3e38
NBR = 3
DIL = ((128, 1), (512, 4), (2048, 16))
BUCKETS, MAX_DIST = 32, 2048
RANK = 256
RC = RANK // P
IDX_HEADS = 8
TOPK = min(256, SEQ // 4)
FF = 2816
FC = FF // P
EXPERTS = 8
FE = 3584
FT = 512
NT = FE // FT
CAP = 128
EXTRA = 2 * SEQ // (CAP + 1)
NPASS = EXPERTS + EXTRA
COLS = NPASS + 1
RING = 7
UNIT = 1024
HALF = 2 * UNIT
SLOTS = 6
OUT_IN_STEP = 5
NARROW = DC * EXPERTS
COPIES = 32
CAUSAL = P + SEQ

C_ID, C_MASK, C_TRI, C_ONES, C_IOTA, C_HOT = 0, 128, 1152, 1280, 1408, 1536
C_N = C_HOT + 384
G_MEM, G_MIX0, G_FFN0, G_MIX1, G_FFN1, G_KV, G_N = 0, 8, 16, 24, 32, 40, 42


def distance_buckets(n):
    half = BUCKETS // 2
    nf = np.maximum(n, 1).astype(np.float32)
    large = half + (np.log(nf / np.float32(half)) / np.float32(math.log(MAX_DIST / half))
                    * np.float32(BUCKETS - half)).astype(np.int32)
    return np.where(n < half, n, np.minimum(large, BUCKETS - 1))


def shape_constants():
    c = np.zeros((P, C_N), np.float32)
    row, col = np.arange(P)[:, None], np.arange(P)[None, :]
    c[:, C_ID:C_ID + P] = row == col
    dist = P + row - np.arange(2 * P)[None, :]
    for b, (window, dilation) in enumerate(DIL):
        seen = (dist >= 0) & (dist <= window) & (dist % dilation == 0)
        c[:, C_MASK + b * 256:C_MASK + (b + 1) * 256] = np.where(seen, 0.0, NEG)
    c[:, C_MASK + 768:C_MASK + 1024] = np.where(dist >= 0, 0.0, NEG)
    c[:, C_TRI:C_TRI + P] = row < col
    c[:, C_ONES:C_ONES + P] = 1.0
    c[:, C_IOTA:C_IOTA + P] = col
    back = np.maximum(255 - np.arange(384), 0)
    c[:BUCKETS, C_HOT:C_HOT + 384] = distance_buckets(back)[None, :] == np.arange(BUCKETS)[:, None]
    return c


ORDER = [("gate", 0), ("up", 0)]
for _j in range(1, NT):
    ORDER += [("gate", _j), ("up", _j), ("down", _j - 1)]
ORDER.append(("down", NT - 1))
TILES = len(ORDER)
PASS_UNITS = 4 * TILES
LAST_TOKENS = 4 * ORDER.index(("up", NT - 1)) + 3

FFN = [("gate", 0), ("up", 0)]
for _c in range(1, FC):
    FFN += [("gate", _c), ("up", _c), ("down", _c - 1)]
FFN.append(("down", FC - 1))
FFN_LOOPS = (FC - 2) // 2


IDX_KEY, IDX_Q, IDX_W, IDX_C = 0, 1, 5, 6


class Units:

    def __init__(self):
        self.slot, self.previous, self.loads, self.at = [], [], [], {}
        last, loaded = [None] * SLOTS, [0] * SLOTS

        def add(key, slot, loads=1):
            self.at[key] = len(self.slot)
            loaded[slot] += loads
            self.previous.append(last[slot])
            self.loads.append(loaded[slot])
            last[slot] = len(self.slot)
            self.slot.append(slot)
        for n in range(8):
            add(("mem", n), n % SLOTS)
        for l in range(2):
            for g in range(PAIRS):
                for m in range((NBR + 2, 3)[l]):
                    add(("pair", l, g, m), m if l == 0 else 3 * (g % 2) + m)
            for j in range(XPAIRS):
                add(("pair", l, PAIRS + j, 0), (5, 0)[j] if l == 0 else (0, 5)[j])
            for ch in range(NPAIR):
                add(("out", l, ch), (ch + 1) % SLOTS)
            if l == 0:
                for n in range(len(FFN)):
                    add(("ffn", n), n % SLOTS)
                for n in range(8):
                    add(("idx", n), n % SLOTS, 2 if n == IDX_KEY else 1)
        add(("router", 0), SLOTS - 1)
        self.count = len(self.slot)


U = Units()
BASE = U.count
assert all(U.slot[BASE - SLOTS + u] == u for u in range(SLOTS)) and PASS_UNITS % SLOTS == 0


def along(i, first, values):
    if isinstance(i, int):
        return values[i - first]
    step = values[1] - values[0]
    assert all(b - a == step for a, b in zip(values, values[1:]))
    return i * step + (values[0] - first * step)


class Pair:

    def __init__(self, l, idx, par, span=None):
        self.l, self.idx, self.par = l, idx, par
        self.span = [idx] if span is None else list(span)
        self.g = 2 * idx + par
        gs = [2 * i + par for i in self.span]
        self.cross = gs[0] >= PAIRS
        self.nbr = 1 if self.cross or l else NBR
        self.kind = "cross" if self.cross else ("even", "odd")[l]
        self.mats = 1 if self.cross else self.nbr + 2
        self.gs = gs

    def value(self, f):
        return along(self.idx, self.span[0], [f(g) for g in self.gs])

    def unit(self, m):
        return [U.at[("pair", self.l, g, m)] for g in self.gs]

    def before(self):
        full = (NBR + 2, 3)[self.l]
        return self.value(lambda g: full * g if g <= PAIRS else full * PAIRS + g - PAIRS)

    def bank(self, m):
        full = (NBR + 2, 3)[self.l]
        g = self.gs[0]
        return 3 + ((full * g if g <= PAIRS else full * PAIRS + g - PAIRS) + m) % 2


def pair_at(l, g):
    return Pair(l, g // 2, g % 2)


def steps(l, engine, one):
    last = PAIRS // 2 - 3
    span = range(0, last + 1)
    with engine.Fori(0, last + 1) as i:
        for par in range(2):
            now = Pair(l, i, par, span)
            nxt = Pair(l, i + (par + 1) // 2, (par + 1) % 2, [k + (par + 1) // 2 for k in span])
            aft = Pair(l, i + 1, par, [k + 1 for k in span])
            one(now, nxt, aft)
    for g in range(2 * (last + 1), NPAIR):
        one(pair_at(l, g), *(pair_at(l, h) if h < NPAIR else None for h in (g + 1, g + 2)))


def build(nc, x, mem, rel_bias, gains, final_norm, consts, w_mem_kv, w_out, even_w_in, even_w_gate,
          even_w_up, even_w_down, odd_w_in, odd_w_uk, odd_w_uv, odd_w_router, odd_w_gate, odd_w_up,
          odd_w_down, out):
    scratch = nc.dram_tensor("bias_rows", [COPIES, HEADS, 384], F32, kind="Internal").ap()

    def rows(w):
        return w.rearrange("(c p) n -> p c n", p=P)

    w_in = (rows(even_w_in[0]), rows(odd_w_in[0]))
    w_kv = (rows(w_mem_kv[0]), rows(w_mem_kv[1]))
    w_o = (rows(w_out[0]), rows(w_out[1]))
    w_uk = rows(odd_w_uk[0].rearrange("r h c -> r (h c)"))
    w_uv = rows(odd_w_uv[0].rearrange("r h c -> r (h c)"))
    ffn_w = {"gate": rows(even_w_gate[0]), "up": rows(even_w_up[0]), "down": rows(even_w_down[0])}
    w_router = rows(odd_w_router[0])
    expert_w = {"gate": odd_w_gate[0].rearrange("e (c p) f -> p (e c) f", p=P),
                "up": odd_w_up[0].rearrange("e (c p) f -> p (e c) f", p=P),
                "down": odd_w_down[0].rearrange("e (c p) n -> p (e c) n", p=P)}
    x_d = x[0].rearrange("(t p) d -> p t d", p=P)
    mem_d = mem[0].rearrange("(t p) d -> p t d", p=P)
    out_d = out[0].rearrange("(t p) d -> p t d", p=P)
    Q_X = (NBR + 2) * D
    O_C, O_QI = D, D + RANK
    O_KI = O_QI + IDX_HEADS * HD
    O_WI = O_KI + HD
    O_X = O_WI + IDX_HEADS

    with ExitStack() as ctx:
        def sb(name, shape, dt=F32):
            return ctx.enter_context(nc.sbuf_tensor(name, shape, dt))

        def sem(name):
            return ctx.enter_context(nc.semaphore(name))

        ps = ctx.enter_context(nc.psum_tensor("ps", [P, 8, 512], F32))
        big = sb("big", [P, RING * HALF])
        raw = [big[:, s * UNIT:(s + 1) * UNIT] for s in range(SLOTS)]
        bmp = big[:, 6144:9216].rearrange("p (r h b s) -> p r h b s", r=2, h=2, b=NBR)
        bias = big[:, 9216:13312].rearrange("p (h s) -> p h s", h=HEADS)
        ring = [big[:, s * HALF:(s + 1) * HALF] for s in range(RING)]
        w_hi = sb("w_hi", [P, SLOTS, UNIT], F32R)
        w_lo = sb("w_lo", [P, SLOTS, UNIT], F32R)
        X = sb("X", [P, TT, D])
        XH = sb("XH", [P, TT, D])
        h_hi = sb("h_hi", [P, DC, SEQ], F32R)
        h_lo = sb("h_lo", [P, DC, SEQ], F32R)
        m_hi = sb("m_hi", [P, NPAIR, SEQ], F32R)
        m_lo = sb("m_lo", [P, NPAIR, SEQ], F32R)
        con = sb("con", [P, C_N])
        gn = sb("gn", [P, G_N])
        relb = sb("relb", [BUCKETS, HEADS])
        z = sb("z", [P, NBR * CAUSAL])
        pr = sb("pr", [P, NBR * CAUSAL])
        tmp = sb("tmp", [P, CAUSAL])
        pn = sb("pn", [P, 512])
        pts = sb("pts", [P, 512])
        qT = sb("qT", [P, 2, NBR, SEQ])
        kT = sb("kT", [P, 2, SEQ])
        vT = sb("vT", [P, SEQ])
        vN = sb("vN", [P, TT, P])
        kx = sb("kx", [P, 2 * XPAIRS, SEQ])
        vx = sb("vx", [P, 2 * XPAIRS, TT, P])
        small = sb("small", [P, 64])
        qiT = sb("qiT", [P, 4, SEQ])
        kiT = sb("kiT", [P, SEQ])
        c_hi = sb("c_hi", [P, RC, SEQ], F32R)
        c_lo = sb("c_lo", [P, RC, SEQ], F32R)
        selm = sb("selm", [P, CAUSAL])
        rt = selm
        itab = sb("itab", [P, 4], I32)
        uidx = sb("uidx", [P, TT, 8], U32)

        nar = vT[0:8, :]
        ebuf = qT[0:HEADS, :, :, :].rearrange("h r b n -> h (r b n)")[:, 0:384]
        ident = con[:, C_ID:C_ID + P]
        tri = con[:, C_TRI:C_TRI + P]
        ones = con[:, C_ONES:C_ONES + P]
        iota = con[:, C_IOTA:C_IOTA + P]
        iota8 = con[:, C_IOTA:C_IOTA + 8]
        causal = con[:, C_MASK + 768:C_MASK + 1024]
        ss, ms, sd, rstd = (small[:, i:i + 2] for i in (0, 2, 4, 6))
        nmx, den, rden = (small[:, i:i + 4].rearrange("p (r t) -> p r t", r=2) for i in (8, 48, 52))
        ms8 = small[:, 16:32].rearrange("p (t k) -> p t k", t=2)
        wis = small[:, 32:48].rearrange("p (t k) -> p t k", t=2)
        cN = pn[:, :].rearrange("p (t r) -> p t r", t=TT)
        rl = z[:, 0:2 * CAUSAL].rearrange("p (r s) -> p r s", r=2)
        scr = pr[:, 0:2 * CAUSAL].rearrange("p (r s) -> p r s", r=2)
        fsg = z[:, 0:512].rearrange("p (r n) -> p r n", r=2)
        fh = pr[:, 0:512].rearrange("p (r n) -> p r n", r=2)
        f_hi, f_lo = c_hi, c_lo
        esg, eh = qT[:, 0, 0:2, :].rearrange("p b n -> p (b n)"), pts[:, :]
        e_hi = h_hi[:, 0:2, :].rearrange("p c n -> p (c n)").rearrange("p (k n) -> p k n", k=4)
        e_lo = h_lo[:, 0:2, :].rearrange("p c n -> p (c n)").rearrange("p (k n) -> p k n", k=4)
        g_hi = m_hi[:, 0:4, :].rearrange("p c n -> p (c n)").rearrange("p (c n) -> p c n", c=DC)
        g_lo = m_lo[:, 0:4, :].rearrange("p c n -> p (c n)").rearrange("p (c n) -> p c n", c=DC)
        ysb = z[:, 0:D]
        fin_gain = qiT[:, :, :].rearrange("p c n -> p (c n)")
        Sg = pn[:, 0:256].rearrange("p (t s) -> p t s", t=TT)
        SG = pn[:, 256:512].rearrange("p (t s) -> p t s", t=TT)
        SGT = kiT[:, :]
        lg, sel, gate_e, oh0, oh1 = (rt[:, i:i + 16].rearrange("p (t k) -> p t k", t=2)
                                     for i in (0, 16, 32, 48, 64))
        top8 = rt[:, 80:96].rearrange("p (t k) -> p t k", t=2)
        idxf = rt[:, 96:112].rearrange("p (t k) -> p t k", t=2)
        slot1 = rt[:, 112:128].rearrange("p (t k) -> p t k", t=2)
        assert COLS <= 12
        slotc = rt[:, 128:152].rearrange("p (t k) -> p t k", t=2)
        gatec = rt[:, 152:176].rearrange("p (t k) -> p t k", t=2)
        dlt, ex2, den2, g1, g2 = (rt[:, i:i + 2] for i in (176, 178, 180, 182, 184))
        over, pa, pb, pc = (rt[:, i:i + 8] for i in (192, 200, 208, 216))
        ind = rt[:, 224:248].rearrange("p (k e) -> p k e", k=EXTRA)
        tabf = rt[:, 256:260]

        s_x, s_con, s_mem, s_rel = map(sem, ("x_in", "consts_in", "mem_in", "rel_in"))
        s_e, s_eb, s_scrw, s_bias, s_bm = map(sem, ("rel_rows", "rel_rows_sb", "rows_out", "bias_in", "bias_masked"))
        s_ss, s_ms, s_sd, s_rstd, s_xh, s_ntr, s_nhi, s_nlo = map(
            sem, ("sum_squares", "mean_square", "root", "rstd", "normalised", "norm_turned", "norm_hi", "norm_lo"))
        s_xr, s_row0 = map(sem, ("residual_added", "row_tile0_complete"))
        s_raw = [sem(f"raw_in{s}") for s in range(SLOTS)]
        s_hi, s_lo, s_used = map(sem, ("unit_hi", "unit_lo", "unit_used"))
        names = ("evacuated", "turned_v", "values", "scores", "scores_read", "masked", "max", "exp",
                 "added", "summed", "probs", "probs_turned", "probsT", "mixed", "mix_hi", "mix_lo", "dve_rden")
        s_at = [{n: sem(f"{n}{l}") for n in names} for l in range(2)]
        s_me, s_mvt, s_mv = map(sem, ("mem_evacuated", "mem_turned", "mem_values"))
        s_fs, s_fh, s_fhi, s_fa = map(sem, ("ffn_silu", "ffn_hidden", "ffn_hidden_hi", "ffn_hidden_lo"))
        s_wi, s_qie, s_wie = map(sem, ("idx_weights_turned", "idx_qk_sb", "idx_weights_sb"))
        s_cch, s_ctr, s_chi, s_clo, s_isc, s_rl, s_acc, s_sel, s_tk = map(
            sem, ("latent_chain", "latent_turned", "latent_hi", "latent_lo", "idx_scores", "idx_relu", "idx_added",
                  "keys_chosen", "topk_chain"))
        s_cnt, s_nar, s_lg, s_ex2, s_rch, s_sl, s_rank, s_tab = map(
            sem, ("counts_read", "narrow_sb", "logits", "gate_exp", "route_chain", "chosen", "ranked", "passes_known"))
        s_ring = [sem(f"ring_in{s}") for s in range(RING)]
        s_S, s_SG, s_gat, s_ghi, s_glo, s_sgt, s_sgte = map(
            sem, ("pick_ready", "put_ready", "gathered", "tokens_hi", "tokens_lo", "put_turned", "putT"))
        s_silu, s_h, s_ht, s_ehi, s_elo, s_y, s_cmb, s_xadd = map(
            sem, ("silu_done", "hidden", "hidden_turned", "hidden_hi", "hidden_lo", "y_out", "combined", "x_added"))
        s_fin, s_out, s_fgin = map(sem, ("final", "stored", "final_gain_in"))

        NORM_MEM, NORM_MIX0, NORM_FFN0, NORM_MIX1, NORM_FFN1, NORM_END = range(6)
        GCOL = (G_MEM, G_MIX0, G_FFN0, G_MIX1, G_FFN1)
        XR = {NORM_MIX0: 0, NORM_FFN0: 2, NORM_MIX1: 4, NORM_FFN1: 6}

        def views(pair, hh):
            n0 = SEQ if pair.cross else P
            w = n0 + SEQ
            o = 512 * hh if pair.nbr == 1 else 0
            return (z[:, o:o + pair.nbr * w].rearrange("p (b s) -> p b s", b=pair.nbr),
                    pr[:, o:o + pair.nbr * w].rearrange("p (b s) -> p b s", b=pair.nbr), n0)

        def score_banks(pair, hh, t):
            if pair.nbr == 1:
                n0 = SEQ if pair.cross else P
                return ps[:, hh, (0, n0)[t]:(n0, n0 + SEQ)[t]].rearrange("p (b s) -> p b s", b=1)
            if t == 0:
                return ps[:, 0, 0:NBR * P].rearrange("p (b s) -> p b s", b=NBR)
            return ps[:, 1:3, :].rearrange("p k n -> p (k n)")[:, 0:NBR * SEQ].rearrange("p (b s) -> p b s", b=NBR)

        def norm_bank(c):
            return ps[:, (0, 1, 5, 6)[c % 4], 0:SEQ]

        def out_banks(t):
            return (ps[:, 2:4, :], ps[:, 4:8:3, :])[t]

        def width(pair, m):
            return RC * P if pair.kind == "odd" and m > 0 else UNIT

        def ring_slot(i):
            return (i + 3) % RING

        def outs(split_unit, now, place):
            if isinstance(now.g, int):
                nexts = [("out", now.l, ch) for ch in range(NPAIR)] + [("ffn", n) for n in range(4 if now.l == 0 else 0)]
                first, count = {(7, 3): (0, 3), (8, 1): (3, 1), (8, 3): (4, 1), (9, 0): (5, 1), (9, 1): (6, 1),
                                (9, 2): (7, 1), (9, 3): (8, 2 + 4 * (now.l == 0))}.get((now.g, place), (0, 0))
                for key in nexts[first:first + count]:
                    split_unit(0, 0, [U.at[key]])

        block = ctx.enter_context(nc.Block())

        @block.sync
        def _(sp):
            def load(i, first, units, src, n=UNIT):
                prev = [U.previous[u] for u in units]
                if prev[0] is not None:
                    sp.wait_ge(s_lo, along(i, first, [p + 1 for p in prev]))
                slot = U.slot[units[0]]
                dst = raw[slot][:, 0:n].rearrange("p (c n) -> p c n", c=src.shape[1])
                sp.dma_start(dst, src).then_inc(s_raw[slot], 16)

            def mat(pair, m):
                l, g = pair.l, pair.g
                if pair.cross:
                    col = (Q_X, O_X)[l] + (g - PAIRS) * P
                    return w_in[l][:, :, col:col + P]
                if l == 0:
                    return w_in[0][:, :, bass.ds(m * D + g * P, P)]
                return (w_in[1], w_uk, w_uv)[m][:, :, bass.ds(g * P, P)]

            def load_pair(pair):
                for m in range(pair.mats):
                    load(pair.idx, pair.span[0], pair.unit(m), mat(pair, m), width(pair, m))

            def stream_loads(l):
                span = range(1, PAIRS // 2)
                load_pair(pair_at(l, 0))
                load_pair(pair_at(l, 1))
                with sp.Fori(1, PAIRS // 2) as i:
                    for par in range(2):
                        load_pair(Pair(l, i, par, span))
                for g in range(PAIRS, NPAIR):
                    load_pair(pair_at(l, g))
                for ch in range(NPAIR):
                    load(0, 0, [U.at[("out", l, ch)]], w_o[l][:, ch:ch + 1, :])

            sp.dma_start(XH[:, :, :], mem_d).then_inc(s_mem, 16)
            sp.dma_start(con[:, :], consts).then_inc(s_con, 16)
            sp.dma_start(relb[:, :], rel_bias).then_inc(s_rel, 16)
            sp.dma_start(gn[:, :], gains).then_inc(s_con, 16)
            for n in range(8):
                if n == 4:
                    sp.dma_start(X[:, :, :], x_d).then_inc(s_x, 16)
                l, q = n // 4, n % 4
                load(0, 0, [U.at[("mem", n)]], w_kv[l][:, :, q * P:(q + 1) * P])
            stream_loads(0)

            def ffn_load(i, first, ns):
                kind, c0 = FFN[ns[0]]
                c = along(i, first, [FFN[n][1] for n in ns])
                src = ffn_w[kind][:, bass.ds(c, 1), :] if kind == "down" else ffn_w[kind][:, :, bass.ds(c * P, P)]
                load(i, first, [U.at[("ffn", n)] for n in ns], src)

            for n in range(8):
                ffn_load(0, 0, [n])
            span = range(1, FFN_LOOPS)
            with sp.Fori(1, FFN_LOOPS) as i:
                for k in range(6):
                    ffn_load(i, 1, [2 + 6 * b + k for b in span])
            for n in range(2 + 6 * FFN_LOOPS, len(FFN)):
                ffn_load(0, 0, [n])

            u = U.at[("idx", IDX_KEY)]
            sp.wait_ge(s_lo, U.previous[u] + 1)
            for half in range(2):
                dst = raw[U.slot[u]].rearrange("p (c n) -> p c n", c=DC)[:, :, half * HD:(half + 1) * HD]
                sp.dma_start(dst, w_in[1][:, :, O_KI:O_KI + HD]).then_inc(s_raw[U.slot[u]], 16)
            for n in range(4):
                load(0, 0, [U.at[("idx", IDX_Q + n)]], w_in[1][:, :, O_QI + n * P:O_QI + (n + 1) * P])
            load(0, 0, [U.at[("idx", IDX_W)]], w_in[1][:, :, O_WI:O_WI + IDX_HEADS], NARROW)
            for n in range(2):
                load(0, 0, [U.at[("idx", IDX_C + n)]], w_in[1][:, 4 * n:4 * n + 4, O_C:O_C + RANK])
            stream_loads(1)

            def half_load(i, e):
                (kind, j), h = ORDER[i // 2], i % 2
                if kind == "down":
                    src = expert_w[kind][:, bass.ds(e * (FE // P) + 4 * j + 2 * h, 2), :]
                else:
                    src = expert_w[kind][:, bass.ds(e * DC + 4 * h, 4), j * FT:(j + 1) * FT]
                s = ring_slot(i)
                dst = ring[s].rearrange("p (c n) -> p c n", c=src.shape[1])
                sp.dma_start(dst, src).then_inc(s_ring[s], 16)

            def half_free(i, before):
                sp.wait_ge(s_lo, before + 2 * (i - RING) + 2)

            load(0, 0, [U.at[("router", 0)]], w_router, NARROW)
            sp.wait_ge(s_at[1]["scores_read"], 2 * PAIRS + 1)
            for i in range(4):
                half_load(i, 0)
            sp.wait_ge(s_lo, BASE)
            for i in range(4, RING):
                half_load(i, 0)
            for i in range(RING, 2 * TILES):
                half_free(i, BASE)
                half_load(i, 0)
            sp.wait_ge(s_isc, IDX_HEADS)
            sp.dma_start(fin_gain, bass.AP(final_norm.tensor, 0, [[0, P], [1, D]])).then_inc(s_fgin, 16)
            with sp.Fori(1, EXPERTS) as p:
                for i in range(2 * TILES):
                    half_free(i, PASS_UNITS * p + BASE)
                    half_load(i, p)
            sp.wait_ge(s_tab, 1)
            n_pass = sp.value_load(itab[0:1, 0:1], min_val=EXPERTS, max_val=NPASS)
            for k in range(EXTRA):
                e = sp.value_load(itab[0:1, 1 + k:2 + k], min_val=0, max_val=EXPERTS - 1)
                with sp.If(n_pass > EXPERTS + k):
                    for i in range(2 * TILES):
                        half_free(i, PASS_UNITS * (EXPERTS + k) + BASE)
                        half_load(i, e)
            sp.wait_ge(s_fin, TT)
            sp.dma_start(out_d, XH[:, :, :]).then_inc(s_out, 16)
            sp.wait_ge(s_out, 16)

        @block.gpsimd
        def _(pool):
            pool.wait_ge(s_eb, 1)
            src = ebuf.rearrange("h (o j) -> h o j", o=1).broadcast_to([HEADS, COPIES, 384])
            pool.dma_start(scratch.rearrange("p h j -> h p j"), src).then_inc(s_scrw, 16)
            pool.wait_ge(s_scrw, 16)
            for p0 in range(0, P, COPIES):
                skew = bass.AP(scratch.tensor, P - 1 - p0, [[HEADS * 384 - 1, COPIES], [384, HEADS], [1, 256]])
                pool.dma_start(bias[p0:p0 + COPIES, :, :], skew).then_inc(s_bias, 16)
            pool.wait_ge(s_bias, 16 * (P // COPIES))
            pool.wait_ge(s_con, 32)

            def mask_pair(g, par, first):
                if not first:
                    pool.wait_ge(s_at[0]["scores_read"], 2 * g - 1)
                for b in range(NBR):
                    m = con[:, C_MASK + b * 256:C_MASK + (b + 1) * 256].rearrange("p (o s) -> p o s", o=1)
                    nc.gpsimd.tensor_tensor(bmp[:, par, :, b, :], bias[:, bass.ds(2 * g, 2), :],
                                            m.broadcast_to([P, 2, 256]), ALU.add).then_inc(s_bm, 1)

            mask_pair(0, 0, True)
            mask_pair(1, 1, True)
            with pool.Fori(1, PAIRS // 2) as i:
                for par in range(2):
                    mask_pair(2 * i + par, par, False)

        @block.tensor
        def _(pe):
            mm, tr = nc.tensor.matmul, nc.tensor.transpose

            def mm3(dst, a, b, start, stop, **kw):
                mm(dst, a[0], b[0], start=start, stop=False, **kw)
                mm(dst, a[0], b[1], start=False, stop=False, **kw)
                return mm(dst, a[1], b[0], start=False, stop=stop, **kw)

            def split(i, first, units, c, n=UNIT):
                pe.wait_ge(s_lo, along(i, first, [u + 1 for u in units]))
                slot = U.slot[units[0]]
                return tuple(w[:, slot, 0:n].rearrange("p (c n) -> p c n", c=c) for w in (w_hi, w_lo))

            def part(pr_, *ix):
                return tuple(a[ix] for a in pr_)

            A_ = slice(None)
            HS, MS, CS = (h_hi, h_lo), (m_hi, m_lo), (c_hi, c_lo)

            def tok(t):
                return slice(t * P, (t + 1) * P)

            def norm_turn(k):
                for c in range(DC):
                    if DC * k + c >= 4:
                        pe.wait_ge(s_nlo, DC * k + c - 3)
                    for t in range(TT):
                        if c == 0:
                            pe.wait_ge(s_xh, TT * k + t + 1)
                        last = tr(norm_bank(c)[:, tok(t)], XH[:, t, c * P:(c + 1) * P], ident)
                    last.then_inc(s_ntr, 1)

            def product(dst, w, src, kc, norm=None):
                for c in range(kc):
                    if norm is not None:
                        pe.wait_ge(s_nlo, DC * norm + c + 1)
                    last = mm3(dst, part(w, A_, c, A_), part(src, A_, c, A_), c == 0, c == kc - 1)
                last.then_inc(s_used, 1)

            def project(pair, m, norm=None):
                S = s_at[pair.l]
                n = pair.before() + m
                if not (isinstance(n, int) and n < 2):
                    pe.wait_ge(S["evacuated"], n - 1)
                src, kc = (CS, RC) if pair.kind == "odd" and m > 0 else (HS, DC)
                if src is CS:
                    pe.wait_ge(s_clo, RC)
                w = split(pair.idx, pair.span[0], pair.unit(m), kc, width(pair, m))
                product(ps[:, pair.bank(m), 0:SEQ], w, src, kc, norm)

            def turn_values(pair):
                S = s_at[pair.l]
                pe.wait_ge(S["evacuated"], pair.before() + pair.mats)
                for t in range(TT):
                    last = tr(ps[:, 7, tok(t)], vT[:, tok(t)], ident)
                last.then_inc(S["turned_v"], 1)

            def keys(pair):
                return kx[:, pair.l * XPAIRS + pair.gs[0] - PAIRS, :] if pair.cross else kT[:, pair.par, :]

            def scores(pair, hh):
                S = s_at[pair.l]
                pe.wait_ge(S["evacuated"], pair.before() + (1 if pair.cross else pair.nbr + 1))
                if pair.l == 0:
                    pe.wait_ge(S["scores_read"], 2 * pair.g + hh + 1)
                elif not (isinstance(pair.g, int) and pair.g == 0):
                    pe.wait_ge(S["scores_read"], 2 * pair.g + hh)
                r = slice(HD * hh, HD * hh + HD)
                k = keys(pair)
                for b in range(pair.nbr):
                    mm(score_banks(pair, hh, 0)[:, b, :], qT[r, pair.par, b, 0:P], k[r, 0:SEQ if pair.cross else P],
                       start=True, stop=True)
                    last = mm(score_banks(pair, hh, 1)[:, b, :], qT[r, pair.par, b, P:SEQ], k[r, :], start=True, stop=True)
                last.then_inc(S["scores"], 1)

            def turn_probs(pair, hh):
                S = s_at[pair.l]
                pe.wait_ge(S["probs"], 2 * pair.g + hh + 1)
                pe.wait_ge(S["probsT"], 2 * pair.g + hh + 1)
                for a, b in ([(0, 0), (1, 2), (2, 1), (3, 3)] if pair.cross else [(0, 0), (1, 1), (2, 2)]):
                    last = tr(ps[:, 5, tok(b)], pn[:, tok(a)], ident)
                last.then_inc(S["probs_turned"], 1)

            def mix(pair, hh):
                S = s_at[pair.l]
                pe.wait_ge(S["probsT"], 2 * pair.g + hh + 2)
                if hh == 0:
                    pe.wait_ge(S["mix_lo"], pair.g + 1)
                    if not pair.cross:
                        pe.wait_ge(S["values"], pair.g + 1)
                o = ps[HD * hh:HD * hh + HD, 6, :]
                v = (vx[:, pair.l * XPAIRS + pair.gs[0] - PAIRS, :, :] if pair.cross else vN[:, :, :])
                v = v[:, :, HD * hh:HD * hh + HD]
                mm(o[:, 0:SEQ], v[:, 0, :], pts[:, 0:SEQ], start=True, stop=False)
                if pair.cross:
                    last = mm(o[:, 0:SEQ], v[:, 1, :], pts[:, SEQ:2 * SEQ], start=False, stop=True)
                else:
                    last = mm(o[:, P:SEQ], v[:, 1, :], pts[:, SEQ:SEQ + P], start=False, stop=True)
                last.then_inc(S["mixed"], 1)

            def out_unit(l, ch):
                if ch == 0:
                    pe.wait_ge(s_at[l]["evacuated"], pair_at(l, NPAIR - 1).before() + 1)
                pe.wait_ge(s_at[l]["mix_lo"], ch + 2)
                w = split(0, 0, [U.at[("out", l, ch)]], 1)
                for t in range(TT):
                    for hf in range(2):
                        last = mm3(out_banks(t)[:, hf, :], part(MS, A_, ch, tok(t)),
                                   part(w, A_, 0, slice(hf * 512, (hf + 1) * 512)), ch == 0, ch == NPAIR - 1,
                                   skip_group_check=True)
                    if ch == NPAIR - 1 and t == 0:
                        last.then_inc(s_row0, 1)
                last.then_inc(s_used, 1)

            def step(now, nxt, aft):
                l = now.l

                def p(*ms):
                    for m in ms:
                        if nxt is None:
                            out_unit(l, m)
                        elif m < nxt.mats:
                            project(nxt, m)
                if not now.cross:
                    turn_values(now)
                if now.kind == "even":
                    p(0)
                    scores(now, 1)
                    p(1)
                    turn_probs(now, 0)
                    p(2, 3)
                    mix(now, 0)
                    turn_probs(now, 1)
                    p(4)
                    scores(nxt, 0)
                    mix(now, 1)
                    return
                scores(now, 1)
                p(0)
                turn_probs(now, 0)
                p(1, 2)
                mix(now, 0)
                if nxt is not None:
                    scores(nxt, 0)
                p(3)
                turn_probs(now, 1)
                p(4)
                mix(now, 1)

            def stream(l, norm=None, behind_queries=None):
                pe.sem_inc(s_at[l]["mixed"], 1)
                pe.sem_inc(s_at[l]["probs_turned"], 1)
                first = pair_at(l, 0)
                for m in range(first.mats):
                    project(first, m, norm if m == 0 else None)
                    if m == 0 and behind_queries is not None:
                        behind_queries()
                scores(first, 0)
                steps(l, pe, step)
                for ch in range(OUT_IN_STEP, NPAIR):
                    out_unit(l, ch)

            pe.wait_ge(s_con, 32)
            pe.wait_ge(s_rel, 16)
            mm(ps[0:HEADS, 2, 0:384], relb[:, :], con[0:BUCKETS, C_HOT:C_HOT + 384], start=True, stop=True).then_inc(s_e, 1)
            norm_turn(NORM_MEM)
            for n in range(8):
                w = split(0, 0, [U.at[("mem", n)]], DC)
                if n >= 2:
                    pe.wait_ge(s_me, n - 1)
                product(ps[:, 3 + n % 2, 0:SEQ], w, MS, DC, NORM_MEM if n == 0 else None)
                if n % 4 >= 2:
                    pe.wait_ge(s_me, n + 1)
                    v = 2 * (n // 4) + n % 2
                    if v:
                        pe.wait_ge(s_mv, v)
                    for t in range(TT):
                        last = tr(ps[:, 7, tok(t)], vT[:, tok(t)], ident)
                    last.then_inc(s_mvt, 1)
                if n == 3:
                    norm_turn(NORM_MIX0)
            pe.wait_ge(s_me, 8)
            pe.wait_ge(s_mv, 4)
            pe.wait_ge(s_eb, 1)
            stream(0, NORM_MIX0)
            norm_turn(NORM_FFN0)

            def ffn_unit(i, first, ns, start=False, stop=False, norm=None):
                kind, c0 = FFN[ns[0]]
                c = along(i, first, [FFN[n][1] for n in ns])
                w = split(i, first, [U.at[("ffn", n)] for n in ns], 1 if kind == "down" else DC)
                par = c0 % 2
                if kind == "down":
                    pe.wait_ge(s_fa, c + 1)
                    for t in range(TT):
                        for hf in range(2):
                            last = mm3(ps[:, 2 * t + hf, :], part((f_hi, f_lo), A_, par, tok(t)),
                                       part(w, A_, 0, slice(hf * 512, (hf + 1) * 512)), start, stop, skip_group_check=True)
                        if stop and t == 0:
                            last.then_inc(s_row0, 1)
                    last.then_inc(s_used, 1)
                    return
                if c0 >= 2:
                    pe.wait_ge(s_fh, c - 1)
                product(ps[:, (4 if kind == "gate" else 6) + par, 0:SEQ], w, HS, DC, norm)

            ffn_unit(0, 0, [0], norm=NORM_FFN0)
            ffn_unit(0, 0, [1])
            for n in range(2, 8):
                ffn_unit(0, 0, [n], start=FFN[n] == ("down", 0))
            span = range(1, FFN_LOOPS)
            with pe.Fori(1, FFN_LOOPS) as i:
                for k in range(6):
                    ffn_unit(i, 1, [2 + 6 * b + k for b in span])
            for n in range(2 + 6 * FFN_LOOPS, len(FFN)):
                ffn_unit(0, 0, [n], stop=FFN[n] == ("down", FC - 1))

            norm_turn(NORM_MIX1)
            w = split(0, 0, [U.at[("idx", IDX_KEY)]], DC)
            product(ps[:, 2, 0:SEQ], w, HS, DC, NORM_MIX1)

            def narrow(u, sb_count):
                product(ps[0:8, 7, 0:SEQ], split(0, 0, [u], DC, NARROW), HS, DC, NORM_FFN1 if sb_count == 2 else None)
                yield
                pe.wait_ge(s_nar, sb_count)
                for t in range(TT):
                    last = tr(ps[:, 7, 256 + t * 8:256 + (t + 1) * 8], nar[:, tok(t)], ident[0:8, 0:8])
                yield last
            for j in range(4):
                w = split(0, 0, [U.at[("idx", IDX_Q + j)]], DC)
                product(ps[:, 3 + j // 2, (j % 2) * SEQ:(j % 2 + 1) * SEQ], w, HS, DC)
            turning = narrow(U.at[("idx", IDX_W)], 1)
            next(turning)

            def latent(n):
                w = split(0, 0, [U.at[("idx", IDX_C + n)]], 4)
                for t in range(TT):
                    for c in range(4):
                        last = mm3(ps[:, 5 + t, 0:RANK], part(HS, A_, 4 * n + c, tok(t)), part(w, A_, c, A_),
                                   n == 0 and c == 0, n == 1 and c == 3, skip_group_check=True)
                last.then_inc(s_used, 1)
            for h in range(IDX_HEADS):
                if h == 2:
                    next(turning).then_inc(s_wi, 1)
                pe.wait_ge(s_qie, 1 + h // 4)
                if h >= 2:
                    pe.wait_ge(s_rl, h - 1)
                r = slice(HD * (h % 2), HD * (h % 2) + HD)
                mm(ps[:, h % 2, 0:P], qiT[r, h // 2, 0:P], kiT[r, 0:P], start=True, stop=True)
                mm(ps[:, h % 2, P:CAUSAL], qiT[r, h // 2, P:SEQ], kiT[r, :], start=True, stop=True).then_inc(s_isc, 1)
            latent(0)
            latent(1)

            def turn_latent():
                pe.wait_ge(s_cch, 4)
                for c in range(RC):
                    for t in range(TT):
                        last = tr(ps[:, 2, c * SEQ + t * P:c * SEQ + (t + 1) * P], cN[:, t, c * P:(c + 1) * P], ident)
                last.then_inc(s_ctr, 1)
            pe.wait_ge(s_rl, IDX_HEADS)
            pe.wait_ge(s_wie, 1)
            stream(1, behind_queries=turn_latent)
            norm_turn(NORM_FFN1)
            turning = narrow(U.at[("router", 0)], 2)
            next(turning)
            next(turning).then_inc(s_lg, 1)
            pe.wait_ge(s_sl, 1)
            mm(ps[:, 6, 0:8], tri, sel[:, 0, :], start=True, stop=True)
            mm(ps[:, 6, 8:16], ones, sel[:, 0, :], start=True, stop=False)
            mm(ps[:, 6, 8:16], tri, sel[:, 1, :], start=False, stop=True)
            mm(ps[:, 6, 16:24], ones, sel[:, 0, :], start=True, stop=False)
            mm(ps[:, 6, 16:24], ones, sel[:, 1, :], start=False, stop=True).then_inc(s_rank, 1)

            def gather(p):
                pe.wait_ge(s_S, p + 1)
                for c in range(DC):
                    for t in range(TT):
                        last = mm(ps[:, 5 + c // 4, (c % 4) * P:(c % 4 + 1) * P], XH[:, t, c * P:(c + 1) * P], Sg[:, t, :],
                                  start=(t == 0), stop=(t == TT - 1))
                    if c % 4 == 3:
                        last.then_inc(s_gat, 1)

            def combine(p):
                pe.wait_ge(s_sgte, p + 1)
                pe.wait_ge(s_y, p + 1)
                for t in range(TT):
                    for hf in range(2):
                        last = mm(ps[:, (5, 2)[t] + hf, :], SGT[:, tok(t)], ysb[:, hf * 512:(hf + 1) * 512],
                                  start=True, stop=True)
                    last.then_inc(s_cmb, 1)

            def expert_unit(u, p):
                (kind, j), q = ORDER[u // 4], u % 4
                pe.wait_ge(s_lo, PASS_UNITS * p + BASE + u + 1)
                slot = u % SLOTS
                c = 1 if kind == "down" else 2
                w = tuple(a[:, slot, :].rearrange("p (c n) -> p c n", c=c) for a in (w_hi, w_lo))
                if kind == "down":
                    if q == 0:
                        pe.wait_ge(s_elo, NT * p + j + 2)
                    for hf in range(2):
                        last = mm3(ps[:, 2 + hf, :], part((e_hi, e_lo), A_, q, A_),
                                   part(w, A_, 0, slice(hf * 512, (hf + 1) * 512)), j == 0 and q == 0, j == NT - 1 and q == 3)
                else:
                    if q == 0:
                        pe.wait_ge(s_silu if kind == "gate" else s_h, NT * p + j + 1)
                    for k in range(2):
                        last = mm3(ps[:, 0 if kind == "gate" else 1, :], part((g_hi, g_lo), A_, 2 * q + k, A_),
                                   part(w, A_, k, A_), q == 0 and k == 0, q == 3 and k == 1)
                last.then_inc(s_used, 1)

            def turn_hidden(j, p):
                pe.wait_ge(s_h, NT * p + j + 2)
                pe.wait_ge(s_elo, NT * p + j + 1)
                for k in range(4):
                    last = tr(ps[:, 4, tok(k)], eh[:, tok(k)], ident)
                last.then_inc(s_ht, 1)

            pe.wait_ge(s_cnt, 1)
            gather(0)
            pe.wait_ge(s_tab, 1)
            n_pass = pe.value_load(itab[0:1, 0:1], min_val=EXPERTS, max_val=NPASS)
            with pe.Fori(0, n_pass) as p:
                pe.wait_ge(s_glo, p + 1)
                for u in range(PASS_UNITS):
                    kind, j = ORDER[u // 4]
                    if u % 4 == 0:
                        if kind == "up" and j:
                            turn_hidden(j - 1, p)
                        if kind == "gate" and j == 1:
                            combine(p)
                        if kind == "down" and j == 0:
                            pe.wait_ge(s_xadd, TT * p + 3)
                        if kind == "down" and j == NT - 2:
                            gather(p + 1)
                            pe.wait_ge(s_SG, p + 1)
                            for t in range(TT):
                                last = tr(ps[:, 7, tok(t)], SG[:, t, :], ident)
                            last.then_inc(s_sgt, 1)
                        if kind == "down" and j == NT - 1:
                            turn_hidden(NT - 1, p)
                    expert_unit(u, p)
            combine(n_pass)

        @block.scalar
        def _(act):
            A = nc.scalar.activation

            def hi(i, first, units, n=UNIT):
                slot = U.slot[units[0]]
                act.wait_ge(s_raw[slot], along(i, first, [16 * U.loads[u] for u in units]))
                prev = [U.previous[u] for u in units]
                if prev[0] is not None:
                    act.wait_ge(s_used, along(i, first, [p + 1 for p in prev]))
                nc.scalar.copy(w_hi[:, slot, 0:n], raw[slot][:, 0:n]).then_inc(s_hi, 1)

            def hi_mat(pair, m):
                if pair is not None and m < pair.mats:
                    hi(pair.idx, pair.span[0], pair.unit(m), width(pair, m))

            def norm_stats(k):
                src = XH if k == NORM_MEM else X
                if k == NORM_MEM:
                    act.wait_ge(s_mem, 16)
                elif k == NORM_MIX0:
                    act.wait_ge(s_x, 16)
                    act.wait_ge(s_rstd, 1)
                if k > NORM_MIX0:
                    A(small[:, 56:57], con[:, C_ONES:C_ONES + 1], ACT.Sqrt)
                if k == NORM_END:
                    act.wait_ge(s_xadd, TT * n_pass_[0] + 3)
                for t in range(TT):
                    if k in XR and XR[k]:
                        act.wait_ge(s_xr, XR[k] - TT + t + 1)
                    last = A((z, pr)[t][:, 0:D], src[:, t, :], ACT.Square, accum_out=ss[:, t:t + 1])
                last.then_inc(s_ss, 1)
                act.wait_ge(s_ms, k + 1)
                A(sd, ms, ACT.Sqrt).then_inc(s_sd, 1)

            def norm_hi(k):
                act.wait_ge(s_con, 32)
                dst = m_hi if k == NORM_MEM else h_hi
                for c in range(DC):
                    act.wait_ge(s_ntr, DC * k + c + 1)
                    A(dst[:, c, :], norm_bank(c), ACT.Copy,
                      scale=gn[:, GCOL[k] + c:GCOL[k] + c + 1]).then_inc(s_nhi, 1)

            def evac(pair, m):
                S = s_at[pair.l]
                if pair is None or m >= pair.mats:
                    return
                act.wait_ge(s_used, along(pair.idx, pair.span[0], [u + 1 for u in pair.unit(m)]))
                if not (isinstance(pair.g, int) and pair.g < 2):
                    act.wait_ge(S["mixed"], 2 * pair.g - 1)
                if not pair.cross and m == pair.nbr + 1 and not (isinstance(pair.g, int) and pair.g < 1):
                    act.wait_ge(S["turned_v"], pair.g)
                dst = qT[:, pair.par, m, :] if m < pair.nbr else kT[:, pair.par, :] if m == pair.nbr else vT[:, :]
                nc.scalar.copy(dst, ps[:, pair.bank(m), 0:SEQ]).then_inc(S["evacuated"], 1)

            def exps(pair, hh):
                S = s_at[pair.l]
                act.wait_ge(S["max"], 2 * pair.g + hh + 1)
                zv, pv, n0 = views(pair, hh)
                for t, (a, b) in enumerate(((0, n0), (n0, n0 + SEQ))):
                    last = A(pv[:, :, a:b], zv[:, :, a:b], ACT.Exp, bias=nmx[:, hh, t:t + 1], accum_out=den[:, hh, t:t + 1])
                last.then_inc(S["exp"], 1)

            def probsT(pair, hh):
                S = s_at[pair.l]
                act.wait_ge(S["probs_turned"], 2 * pair.g + hh + 2)
                act.wait_ge(S["mixed"], 2 * pair.g + hh + 1)
                n = 512 if pair.cross else CAUSAL
                nc.scalar.copy(pts[:, 0:n], ps[:, 5, 0:n]).then_inc(S["probsT"], 1)

            def step(now, nxt, aft):
                S = s_at[now.l]

                def e(m):
                    if nxt is not None and m < nxt.mats:
                        evac(nxt, m)
                if not now.cross:
                    act.wait_ge(S["turned_v"], now.g + 1)
                    nc.scalar.copy(vN[:, :, :].rearrange("p t n -> p (t n)"), ps[:, 7, 0:SEQ]).then_inc(S["values"], 1)
                exps(now, 0)
                if now.kind == "even":
                    e(0)
                    hi_mat(aft, 0)
                    e(1)
                    hi_mat(aft, 1)
                    exps(now, 1)
                    probsT(now, 0)
                    e(2)
                    hi_mat(aft, 2)
                    e(3)
                    hi_mat(aft, 3)
                    probsT(now, 1)
                    e(4)
                    hi_mat(aft, 4)
                else:
                    hi_mat(aft, 0)
                    outs(hi, now, 0)
                    exps(now, 1)
                    e(0)
                    probsT(now, 0)
                    outs(hi, now, 1)
                    e(1)
                    e(2)
                    hi_mat(aft, 1)
                    hi_mat(aft, 2)
                    probsT(now, 1)
                    outs(hi, now, 2)
                act.wait_ge(S["mixed"], 2 * now.g + 3)
                nc.scalar.copy(m_hi[:, bass.ds(now.g, 1), :].rearrange("p o n -> p (o n)"), ps[:, 6, 0:SEQ]).then_inc(S["mix_hi"], 1)
                outs(hi, now, 3)

            def stream(l, done):
                act.sem_inc(s_at[l]["probsT"], 1)
                a, b = pair_at(l, 0), pair_at(l, 1)
                for m in range(done, a.mats):
                    hi_mat(a, m)
                for m in range(a.mats):
                    evac(a, m)
                    hi_mat(b, m)
                steps(l, act, step)

            norm_stats(NORM_MEM)
            act.wait_ge(s_e, 1)
            nc.scalar.copy(ebuf, ps[0:HEADS, 2, 0:384]).then_inc(s_eb, 1)
            hi(0, 0, [U.at[("mem", 0)]])
            norm_hi(NORM_MEM)
            for n in range(1, SLOTS):
                hi(0, 0, [U.at[("mem", n)]])
            norm_stats(NORM_MIX0)
            for n in range(8):
                act.wait_ge(s_used, U.at[("mem", n)] + 1)
                q = 2 * (n // 4) + n % 2
                if n % 4 < 2:
                    nc.scalar.copy(kx[:, q, :], ps[:, 3 + n % 2, 0:SEQ]).then_inc(s_me, 1)
                else:
                    if q:
                        act.wait_ge(s_mvt, q)
                    nc.scalar.copy(vT[:, :], ps[:, 3 + n % 2, 0:SEQ]).then_inc(s_me, 1)
                    if n == 7:
                        hi_mat(pair_at(0, 0), 1)
                        hi_mat(pair_at(0, 0), 2)
                    act.wait_ge(s_mvt, q + 1)
                    nc.scalar.copy(vx[:, q, :, :].rearrange("p t n -> p (t n)"), ps[:, 7, 0:SEQ]).then_inc(s_mv, 1)
                if n + SLOTS < 8:
                    hi(0, 0, [U.at[("mem", n + SLOTS)]])
                if n == 3:
                    norm_hi(NORM_MIX0)
                if n == 6:
                    hi_mat(pair_at(0, 0), 0)
            act.wait_ge(s_scrw, 16)
            stream(0, 3)
            norm_stats(NORM_FFN0)
            for n in range(4, SLOTS):
                hi(0, 0, [U.at[("ffn", n)]])
            norm_hi(NORM_FFN0)

            def silu(i, first, ns):
                if FFN[ns[0]][0] != "gate":
                    return
                c0 = FFN[ns[0]][1]
                c = along(i, first, [FFN[n][1] for n in ns])
                act.wait_ge(s_used, along(i, first, [U.at[("ffn", n)] + 1 for n in ns]))
                if c0 >= 2:
                    act.wait_ge(s_fh, c - 1)
                A(fsg[:, c0 % 2, :], ps[:, 4 + c0 % 2, 0:SEQ], ACT.Silu).then_inc(s_fs, 1)

            def after_unit(n):
                return U.at[("ffn", n)] + SLOTS

            for n in range(8):
                silu(0, 0, [n])
                hi(0, 0, [after_unit(n)])
            span = range(1, FFN_LOOPS - 1)
            with act.Fori(1, FFN_LOOPS - 1) as i:
                for k in range(6):
                    ns = [2 + 6 * b + k for b in span]
                    silu(i, 1, ns)
                    hi(i, 1, [after_unit(n) for n in ns])
            for n in range(2 + 6 * (FFN_LOOPS - 1), len(FFN)):
                silu(0, 0, [n])
                if n < len(FFN) - 1:
                    hi(0, 0, [after_unit(n)])
            norm_stats(NORM_MIX1)
            hi(0, 0, [U.at[("idx", IDX_W)]], NARROW)
            norm_hi(NORM_MIX1)
            for n in range(SLOTS, 8):
                hi(0, 0, [U.at[("idx", n)]])

            def narrow_out(u, count):
                act.wait_ge(s_used, u + 1)
                nc.scalar.copy(nar, ps[0:8, 7, 0:SEQ]).then_inc(s_nar, 1)
            act.wait_ge(s_used, U.at[("idx", IDX_KEY)] + 1)
            nc.scalar.copy(kiT[:, :], ps[:, 2, 0:SEQ])
            for j in range(2):
                act.wait_ge(s_used, U.at[("idx", IDX_Q + 2 * j + 1)] + 1)
                nc.scalar.copy(qiT[:, 2 * j:2 * j + 2, :].rearrange("p a n -> p (a n)"), ps[:, 3 + j, :]).then_inc(s_qie, 1)
            narrow_out(U.at[("idx", IDX_W)], 1)
            for h in range(IDX_HEADS):
                act.wait_ge(s_isc, h + 1)
                if h >= 2:
                    act.wait_ge(s_acc, h - 1)
                A(rl[:, h % 2, :], ps[:, h % 2, 0:CAUSAL], ACT.Relu, scale=HD ** -0.5).then_inc(s_rl, 1)
            hi_mat(pair_at(1, 0), 0)
            act.wait_ge(s_used, U.at[("idx", IDX_C + 1)] + 1)
            for t in range(TT):
                last = A((tmp, pts)[t][:, 0:RANK], ps[:, 5 + t, 0:RANK], ACT.Square, accum_out=ss[:, t:t + 1])
            last.then_inc(s_cch, 1)
            hi_mat(pair_at(1, 0), 1)
            hi_mat(pair_at(1, 0), 2)
            act.wait_ge(s_cch, 2)
            A(sd, ms, ACT.Sqrt).then_inc(s_cch, 1)
            act.wait_ge(s_ctr, 1)
            for c in range(RC):
                A(c_hi[:, c, :], ps[:, 2, c * SEQ:(c + 1) * SEQ], ACT.Copy, scale=gn[:, G_KV + c:G_KV + c + 1]).then_inc(s_chi, 1)
            stream(1, 3)
            hi(0, 0, [U.at[("router", 0)]], NARROW)
            norm_stats(NORM_FFN1)
            norm_hi(NORM_FFN1)
            narrow_out(U.at[("router", 0)], 2)

            def expert_hi(u, p, before=None):
                i, slot = u // 2, u % SLOTS
                s = ring_slot(i)
                act.wait_ge(s_ring[s], 16 * (2 * TILES // RING * p + i // RING + 1))
                act.wait_ge(s_used, PASS_UNITS * p + BASE + u - SLOTS + 1)
                nc.scalar.copy(w_hi[:, slot, :], ring[s][:, (u % 2) * UNIT:(u % 2 + 1) * UNIT]).then_inc(s_hi, 1)

            act.wait_ge(s_rch, 1)
            A(ex2, dlt, ACT.Exp).then_inc(s_ex2, 1)
            act.sem_inc(s_silu, 1)

            def gathered(p):
                for c in range(DC):
                    if c % 4 == 0:
                        act.wait_ge(s_gat, 2 * p + c // 4 + 1)
                    last = A(g_hi[:, c, :], ps[:, 5 + c // 4, (c % 4) * P:(c % 4 + 1) * P], ACT.Copy,
                             scale=gn[:, G_FFN1 + c:G_FFN1 + c + 1])
                    if c % 4 == 3:
                        last.then_inc(s_ghi, 1)

            def hidden_hi(j, p):
                act.wait_ge(s_ht, NT * p + j + 1)
                nc.scalar.copy(e_hi.rearrange("p k n -> p (k n)"), ps[:, 4, :]).then_inc(s_ehi, 1)

            def y_out(need):
                act.wait_ge(s_used, need)
                nc.scalar.copy(ysb, ps[:, 2:4, :].rearrange("p k n -> p (k n)")).then_inc(s_y, 1)

            gathered(0)
            act.wait_ge(s_tab, 1)
            n_pass = act.value_load(itab[0:1, 0:1], min_val=EXPERTS, max_val=NPASS)
            n_pass_ = [n_pass]
            with act.Fori(0, n_pass) as p:
                for u in range(PASS_UNITS):
                    v = u - SLOTS
                    if u == 5:
                        y_out(PASS_UNITS * p + BASE)
                    if v >= 0 and v % 4 == 3:
                        kind, j = ORDER[v // 4]
                        if kind == "gate":
                            if j:
                                hidden_hi(j - 1, p)
                            act.wait_ge(s_used, PASS_UNITS * p + BASE + v + 1)
                            act.wait_ge(s_h, NT * p + j + 1)
                            A(esg, ps[:, 0, :], ACT.Silu).then_inc(s_silu, 1)
                    if v == LAST_TOKENS:
                        gathered(p + 1)
                        act.wait_ge(s_sgt, p + 1)
                        nc.scalar.copy(SGT, ps[:, 7, 0:256]).then_inc(s_sgte, 1)
                    expert_hi(u, p)
                hidden_hi(NT - 1, p)
            y_out(PASS_UNITS * n_pass + BASE)
            norm_stats(NORM_END)

        @block.vector
        def _(dve):
            V = nc.vector

            def rest(dst, src, lead):
                return V.tensor_tensor(dst, src, lead.bitcast(F32), ALU.subtract)

            def lo(i, first, units, n=UNIT):
                slot = U.slot[units[0]]
                dve.wait_ge(s_hi, along(i, first, [u + 1 for u in units]))
                rest(w_lo[:, slot, 0:n], raw[slot][:, 0:n], w_hi[:, slot, 0:n]).then_inc(s_lo, 1)

            def lo_mat(pair, m):
                if pair is not None and m < pair.mats:
                    lo(pair.idx, pair.span[0], pair.unit(m), width(pair, m))

            def rest_scaled(dst, src, gain, lead):
                return V.scalar_tensor_tensor(out=dst, in0=src, scalar=gain, in1=lead.bitcast(F32),
                                              op0=ALU.mult, op1=ALU.subtract)

            def norm_rows(k):
                src = XH if k == NORM_MEM else X
                dve.wait_ge(s_ss, k + 1)
                V.tensor_scalar(ms, ss, 1.0 / D, EPS, ALU.mult, ALU.add).then_inc(s_ms, 1)
                dve.wait_ge(s_sd, k + 1)
                V.reciprocal(rstd, sd).then_inc(s_rstd, 1)
                dve.wait_ge(s_rstd, k + 1)
                if k == NORM_MIX0:
                    dve.wait_ge(s_ntr, DC)
                for t in range(TT):
                    V.tensor_scalar(XH[:, t, :], src[:, t, :], rstd[:, t:t + 1], None, ALU.mult).then_inc(s_xh, 1)

            def norm_lo(k):
                hi_, lo_ = (m_hi, m_lo) if k == NORM_MEM else (h_hi, h_lo)
                for c in range(DC):
                    dve.wait_ge(s_nhi, DC * k + c + 1)
                    rest_scaled(lo_[:, c, :], norm_bank(c), gn[:, GCOL[k] + c:GCOL[k] + c + 1],
                                hi_[:, c, :]).then_inc(s_nlo, 1)

            def head_scores(pair, hh):
                S = s_at[pair.l]
                n = 2 * pair.g + hh
                zv, pv, n0 = views(pair, hh)
                dve.wait_ge(S["scores"], n + 1)
                if pair.kind == "even" and hh == 0:
                    dve.wait_ge(s_bm, NBR * pair.g + NBR)
                tiles = ((0, n0), (n0, n0 + SEQ))
                for t, (a, b) in enumerate(tiles):
                    src = score_banks(pair, hh, t)
                    if pair.cross:
                        last = V.tensor_scalar(zv[:, :, a:b], src, SCALE, None, ALU.mult)
                        continue
                    cols = slice(P, SEQ) if t == 0 else slice(0, SEQ)
                    add = bmp[:, pair.par, hh, :, cols] if pair.l == 0 else bias[:, bass.ds(n, 1), cols]
                    last = V.scalar_tensor_tensor(out=zv[:, :, a:b], in0=src, scalar=SCALE, in1=add,
                                                  op0=ALU.mult, op1=ALU.add)
                last.then_inc(S["scores_read"], 1)
                dve.wait_ge(S["scores_read"], n + 2)
                if pair.kind == "odd":
                    V.tensor_tensor(zv[:, 0, :], zv[:, 0, :], selm[:, :], ALU.add).then_inc(S["masked"], 1)
                    dve.wait_ge(S["masked"], n + 1)
                for t, (a, b) in enumerate(tiles):
                    last = V.tensor_reduce(nmx[:, hh, t:t + 1], zv[:, :, a:b], mybir.AxisListType.XY, ALU.max, negate=True)
                last.then_inc(S["max"], 1)

            def head_probs(pair, hh):
                S = s_at[pair.l]
                n = 2 * pair.g + hh
                zv, pv, n0 = views(pair, hh)
                dve.wait_ge(S["exp"], n + 1)
                V.reciprocal(rden[:, hh, :], den[:, hh, :]).then_inc(S["dve_rden"], 1)
                src = pv[:, 0, :]
                if pair.nbr == NBR:
                    V.tensor_tensor(tmp[:, :], pv[:, 0, :], pv[:, 1, :], ALU.add).then_inc(S["added"], 1)
                    dve.wait_ge(S["added"], n + 1)
                    V.tensor_tensor(tmp[:, :], tmp[:, :], pv[:, 2, :], ALU.add).then_inc(S["summed"], 1)
                    dve.wait_ge(S["summed"], n + 1)
                    src = tmp[:, :]
                dve.wait_ge(S["dve_rden"], n + 1)
                dve.wait_ge(S["probs_turned"], n + 1)
                for t, (a, b) in enumerate(((0, n0), (n0, n0 + SEQ))):
                    last = V.tensor_scalar(pn[:, a:b], src[:, a:b], rden[:, hh, t:t + 1], None, ALU.mult)
                last.then_inc(S["probs"], 1)

            def step(now, nxt, aft):
                S = s_at[now.l]
                if now.kind == "even":
                    head_probs(now, 0)
                    head_scores(now, 1)
                    lo_mat(aft, 0)
                    lo_mat(aft, 1)
                    head_probs(now, 1)
                    for m in range(2, 5):
                        lo_mat(aft, m)
                else:
                    head_scores(now, 1)
                    head_probs(now, 0)
                    lo_mat(aft, 0)
                    outs(lo, now, 0)
                    outs(lo, now, 1)
                    head_probs(now, 1)
                    lo_mat(aft, 1)
                    lo_mat(aft, 2)
                    outs(lo, now, 2)
                if nxt is not None:
                    head_scores(nxt, 0)
                dve.wait_ge(S["mix_hi"], now.g + 1)
                rest(m_lo[:, bass.ds(now.g, 1), :].rearrange("p o n -> p (o n)"), ps[:, 6, 0:SEQ],
                     m_hi[:, bass.ds(now.g, 1), :].rearrange("p o n -> p (o n)")).then_inc(S["mix_lo"], 1)
                outs(lo, now, 3)

            def stream(l):
                dve.sem_inc(s_at[l]["scores_read"], 1)
                dve.sem_inc(s_at[l]["mix_lo"], 1)
                if l == 1:
                    choose_keys()
                else:
                    for m in range(pair_at(l, 0).mats):
                        lo_mat(pair_at(l, 0), m)
                for m in range(pair_at(l, 1).mats):
                    lo_mat(pair_at(l, 1), m)
                head_scores(pair_at(l, 0), 0)
                steps(l, dve, step)

            def residual(n, need, banks):
                for t in range(TT):
                    if t == 0:
                        dve.wait_ge(s_row0, n)
                    else:
                        dve.wait_ge(s_used, need)
                    Xt = X[:, t, :].rearrange("p (k n) -> p k n", k=2)
                    V.tensor_tensor(Xt, Xt, banks(t), ALU.add).then_inc(s_xr, 1)

            norm_rows(NORM_MEM)
            lo(0, 0, [U.at[("mem", 0)]])
            norm_lo(NORM_MEM)
            for n in range(1, SLOTS):
                lo(0, 0, [U.at[("mem", n)]])
            norm_rows(NORM_MIX0)
            for n in range(SLOTS, 8):
                lo(0, 0, [U.at[("mem", n)]])
            norm_lo(NORM_MIX0)
            stream(0)
            residual(1, U.at[("out", 0, NPAIR - 1)] + 1, out_banks)
            norm_rows(NORM_FFN0)
            for n in range(4, SLOTS):
                lo(0, 0, [U.at[("ffn", n)]])
            norm_lo(NORM_FFN0)

            def hidden(i, first, ns):
                if FFN[ns[0]][0] != "up":
                    return
                c0 = FFN[ns[0]][1]
                par = c0 % 2
                c = along(i, first, [FFN[n][1] for n in ns])
                dve.wait_ge(s_fs, c + 1)
                dve.wait_ge(s_used, along(i, first, [U.at[("ffn", n)] + 1 for n in ns]))
                V.tensor_tensor(fh[:, par, :], fsg[:, par, :], ps[:, 6 + par, 0:SEQ], ALU.mult).then_inc(s_fh, 1)
                dve.wait_ge(s_fh, c + 1)
                V.tensor_copy(f_hi[:, par, :], fh[:, par, :]).then_inc(s_fhi, 1)
                dve.wait_ge(s_fhi, c + 1)
                rest(f_lo[:, par, :], fh[:, par, :], f_hi[:, par, :]).then_inc(s_fa, 1)

            def after_unit(n):
                return U.at[("ffn", n)] + SLOTS

            for n in range(8):
                hidden(0, 0, [n])
                lo(0, 0, [after_unit(n)])
            span = range(1, FFN_LOOPS - 1)
            with dve.Fori(1, FFN_LOOPS - 1) as i:
                for k in range(6):
                    ns = [2 + 6 * b + k for b in span]
                    hidden(i, 1, ns)
                    lo(i, 1, [after_unit(n) for n in ns])
            for n in range(2 + 6 * (FFN_LOOPS - 1), len(FFN)):
                hidden(0, 0, [n])
                if n < len(FFN) - 1:
                    lo(0, 0, [after_unit(n)])
            residual(2, U.at[("ffn", len(FFN) - 1)] + 1, lambda t: ps[:, 2 * t:2 * t + 2, :])
            norm_rows(NORM_MIX1)
            lo(0, 0, [U.at[("idx", IDX_W)]], NARROW)
            norm_lo(NORM_MIX1)
            for n in range(SLOTS, 8):
                lo(0, 0, [U.at[("idx", n)]])

            dve.wait_ge(s_wi, 1)
            V.tensor_scalar(wis, ps[:, 7, 256:272].rearrange("p (t k) -> p t k", t=TT), IDX_HEADS ** -0.5, None,
                            ALU.mult).then_inc(s_wie, 1)
            dve.wait_ge(s_wie, 1)
            tiles = ((0, P), (P, CAUSAL))
            for h in range(IDX_HEADS):
                dve.wait_ge(s_rl, h + 1)
                if h:
                    dve.wait_ge(s_acc, h)
                for t, (a, b) in enumerate(tiles):
                    w = wis[:, t, h:h + 1]
                    if h == 0:
                        last = V.tensor_scalar(scr[:, 0, a:b], rl[:, 0, a:b], w, None, ALU.mult)
                    else:
                        last = V.scalar_tensor_tensor(out=scr[:, 0, a:b], in0=rl[:, h % 2, a:b], scalar=w,
                                                      in1=scr[:, 0, a:b], op0=ALU.mult, op1=ALU.add)
                last.then_inc(s_acc, 1)

            def meanwhile(k):
                if k == 2:
                    lo_mat(pair_at(1, 0), 0)
                if k == 4:
                    dve.wait_ge(s_cch, 1)
                    V.tensor_scalar(ms, ss, 1.0 / RANK, EPS, ALU.mult, ALU.add).then_inc(s_cch, 1)
                    lo_mat(pair_at(1, 0), 1)
                    lo_mat(pair_at(1, 0), 2)
                if k == 5:
                    dve.wait_ge(s_cch, 3)
                    V.reciprocal(rstd, sd).then_inc(s_wie, 1)
                    dve.wait_ge(s_wie, 2)
                    for t in range(TT):
                        last = V.tensor_scalar(cN[:, t, :], ps[:, 5 + t, 0:RANK], rstd[:, t:t + 1], None, ALU.mult)
                    last.then_inc(s_cch, 1)
                if k == 7:
                    dve.wait_ge(s_chi, RC)
                    for c in range(RC):
                        rest_scaled(c_lo[:, c, :], ps[:, 2, c * SEQ:(c + 1) * SEQ], gn[:, G_KV + c:G_KV + c + 1],
                                    c_hi[:, c, :]).then_inc(s_clo, 1)
            TOPK_STEPS = 2 * (TOPK // 8) + 1

            def choose_keys():
                tiles = ((0, P), (P, CAUSAL))
                dve.wait_ge(s_acc, IDX_HEADS)
                V.tensor_tensor(scr[:, 1, 0:P], scr[:, 0, 0:P], causal[:, P:SEQ], ALU.add)
                V.tensor_tensor(scr[:, 1, P:CAUSAL], scr[:, 0, P:CAUSAL], causal, ALU.add).then_inc(s_tk, 1)
                cur, n = 1, 1
                for k in range(TOPK // 8):
                    meanwhile(k)
                    dve.wait_ge(s_tk, n)
                    for t, (a, b) in enumerate(tiles):
                        last = V.max(ms8[:, t, :], scr[:, cur, a:b])
                    last.then_inc(s_tk, 1)
                    dve.wait_ge(s_tk, n + 1)
                    for t, (a, b) in enumerate(tiles):
                        last = V.match_replace(scr[:, 1 - cur, a:b], ms8[:, t, :], scr[:, cur, a:b], TAKEN)
                    last.then_inc(s_tk, 1)
                    cur, n = 1 - cur, n + 2
                dve.wait_ge(s_tk, n)
                V.tensor_scalar(scr[:, 1 - cur, :], scr[:, cur, :], -1e35, NEG, ALU.is_gt, ALU.mult).then_inc(s_tk, 1)
                dve.wait_ge(s_tk, n + 1)
                V.tensor_tensor(selm[:, 0:P], scr[:, 1 - cur, 0:P], causal[:, P:SEQ], ALU.add)
                V.tensor_tensor(selm[:, P:CAUSAL], scr[:, 1 - cur, P:CAUSAL], causal, ALU.add).then_inc(s_sel, 1)
                dve.wait_ge(s_sel, 1)
            stream(1)
            lo(0, 0, [U.at[("router", 0)]], NARROW)
            residual(3, U.at[("out", 1, NPAIR - 1)] + 1, out_banks)
            norm_rows(NORM_FFN1)
            norm_lo(NORM_FFN1)

            chain = [0]

            def link(ins):
                chain[0] += 1
                ins.then_inc(s_rch, 1)
                dve.wait_ge(s_rch, chain[0])

            dve.wait_ge(s_lg, 1)
            V.tensor_copy(lg, ps[:, 7, 256:272].rearrange("p (t k) -> p t k", t=TT)).then_inc(s_tk, 1)
            n = TOPK_STEPS + 2
            dve.wait_ge(s_tk, n)
            for t in range(TT):
                last = V.max(top8[:, t, :], lg[:, t, :])
            last.then_inc(s_tk, 1)
            dve.wait_ge(s_tk, n + 1)
            V.tensor_tensor(dlt, top8[:, :, 1], top8[:, :, 0], ALU.subtract)
            V.memset(slotc, -1.0)
            V.memset(gatec, 0.0)
            for t in range(TT):
                last = V.max_index(uidx[:, t, :], top8[:, t, :], lg[:, t, :])
            link(last)
            link(V.tensor_copy(idxf, uidx[:, :, :]))
            for t in range(TT):
                V.tensor_scalar(oh0[:, t, :], iota8, idxf[:, t, 0:1], None, ALU.is_equal)
                last = V.tensor_scalar(oh1[:, t, :], iota8, idxf[:, t, 1:2], None, ALU.is_equal)
            link(last)
            V.tensor_tensor(sel, oh0, oh1, ALU.add).then_inc(s_sl, 1)
            dve.wait_ge(s_rank, 1)
            rank = ps[:, 6, 0:16].rearrange("p (t k) -> p t k", t=TT)
            link(V.scalar_tensor_tensor(out=slot1, in0=rank, scalar=1.0, in1=sel, op0=ALU.add, op1=ALU.mult))
            link(V.tensor_scalar(slotc[:, :, 0:EXPERTS], slot1, 1.0, None, ALU.subtract))

            def pick(p):
                for t in range(TT):
                    at = slotc[:, t, p:p + 1] if isinstance(p, int) else slotc[:, t, bass.ds(p, 1)]
                    last = V.tensor_scalar(Sg[:, t, :], iota, at, None, ALU.is_equal)
                last.then_inc(s_S, 1)
            pick(0)

            V.tensor_scalar(over, ps[:, 6, 16:24], CAP + 0.5, None, ALU.is_gt).then_inc(s_cnt, 1)
            dve.wait_ge(s_ex2, 1)
            link(V.tensor_scalar(den2, ex2, 1.0, None, ALU.add))
            V.tensor_copy(pa[:, 0:1], over[:, 0:1])
            V.tensor_tensor(pa[:, 1:8], over[:, 1:8], over[:, 0:7], ALU.add)
            link(V.reciprocal(g1, den2))
            V.tensor_copy(pb[:, 0:2], pa[:, 0:2])
            V.tensor_tensor(pb[:, 2:8], pa[:, 2:8], pa[:, 0:6], ALU.add)
            for t in range(TT):
                V.tensor_scalar(gate_e[:, t, :], oh0[:, t, :], g1[:, t:t + 1], None, ALU.mult)
            link(V.tensor_tensor(g2, ex2, g1, ALU.mult))
            V.tensor_copy(pc[:, 0:4], pb[:, 0:4])
            V.tensor_tensor(pc[:, 4:8], pb[:, 4:8], pb[:, 0:4], ALU.add)
            for t in range(TT):
                last = V.scalar_tensor_tensor(out=gatec[:, t, 0:EXPERTS], in0=oh1[:, t, :], scalar=g2[:, t:t + 1],
                                              in1=gate_e[:, t, :], op0=ALU.mult, op1=ALU.add)
            link(last)
            for k in range(EXTRA):
                V.scalar_tensor_tensor(out=ind[:, k, :], in0=pc, scalar=k + 1.0, in1=over,
                                       op0=ALU.is_equal, op1=ALU.mult)
            link(V.tensor_scalar(tabf[:, 0:1], pc[:, 7:8], float(EXPERTS), None, ALU.add))

            junks = [0]

            def summed(a, add, b, into):
                junk = tmp[:, junks[0]:junks[0] + 8]
                junks[0] += 8
                return V.scalar_tensor_tensor(out=junk, in0=a, scalar=1.0 if add is None else add, in1=b,
                                              op0=ALU.mult if add is None else ALU.add, op1=ALU.mult, accum_out=into)
            for k in range(EXTRA):
                summed(iota8, None, ind[:, k, :], tabf[:, 1 + k:2 + k])
                for t in range(TT):
                    col = slice(EXPERTS + k, EXPERTS + k + 1)
                    summed(slot1[:, t, :], 4.0 * SEQ, ind[:, k, :], slotc[:, t, col])
                    last = summed(gatec[:, t, 0:EXPERTS], None, ind[:, k, :], gatec[:, t, col])
            link(last)
            link(V.tensor_scalar(slotc[:, :, EXPERTS:NPASS], slotc[:, :, EXPERTS:NPASS], 4.0 * SEQ + 1 + CAP, None,
                                 ALU.subtract))
            V.tensor_copy(itab[:, :], tabf).then_inc(s_tab, 1)

            V.memset(SGT, 0.0).then_inc(s_sgte, 1)
            dve.sem_inc(s_h, 1)
            dve.sem_inc(s_elo, 1)
            dve.sem_inc(s_xadd, 1)

            def expert_lo(u, p):
                i, slot = u // 2, u % SLOTS
                dve.wait_ge(s_hi, PASS_UNITS * p + BASE + u + 1)
                rest(w_lo[:, slot, :], ring[ring_slot(i)][:, (u % 2) * UNIT:(u % 2 + 1) * UNIT], w_hi[:, slot, :]).then_inc(s_lo, 1)

            def gathered(p):
                for c in range(DC):
                    if c % 4 == 0:
                        dve.wait_ge(s_ghi, 2 * p + c // 4 + 1)
                    last = rest_scaled(g_lo[:, c, :], ps[:, 5 + c // 4, (c % 4) * P:(c % 4 + 1) * P],
                                       gn[:, G_FFN1 + c:G_FFN1 + c + 1], g_hi[:, c, :])
                last.then_inc(s_glo, 1)

            def hidden_lo(j, p):
                dve.wait_ge(s_ehi, NT * p + j + 1)
                rest(e_lo.rearrange("p k n -> p (k n)"), ps[:, 4, :], e_hi.rearrange("p k n -> p (k n)")).then_inc(s_elo, 1)

            def add_rows(p):
                for t in range(TT):
                    dve.wait_ge(s_cmb, TT * p + t + 1)
                    b0 = (5, 2)[t]
                    V.tensor_tensor(X[:, t, :], X[:, t, :], ps[:, b0:b0 + 2, :].rearrange("p k n -> p (k n)"),
                                    ALU.add).then_inc(s_xadd, 1)

            gathered(0)
            dve.wait_ge(s_tab, 1)
            n_pass = dve.value_load(itab[0:1, 0:1], min_val=EXPERTS, max_val=NPASS)
            with dve.Fori(0, n_pass) as p:
                for u in range(PASS_UNITS):
                    v = u - SLOTS
                    if v >= 0 and v % 4 == 3:
                        kind, j = ORDER[v // 4]
                        if kind == "gate" and j:
                            hidden_lo(j - 1, p)
                        if kind == "up":
                            dve.wait_ge(s_silu, NT * p + j + 2)
                            dve.wait_ge(s_used, PASS_UNITS * p + BASE + v + 1)
                            V.tensor_tensor(eh, esg, ps[:, 1, :], ALU.mult).then_inc(s_h, 1)
                            if j == 0:
                                dve.wait_ge(s_S, p + 1)
                                for t in range(TT):
                                    last = V.tensor_scalar(SG[:, t, :], Sg[:, t, :], gatec[:, t, bass.ds(p, 1)], None, ALU.mult)
                                last.then_inc(s_SG, 1)
                            if j == 1:
                                dve.wait_ge(s_SG, p + 1)
                                pick(p + 1)
                    if u == 15:
                        add_rows(p)
                    if v == LAST_TOKENS:
                        gathered(p + 1)
                    expert_lo(u, p)
                hidden_lo(NT - 1, p)
            add_rows(n_pass)
            norm_rows(NORM_END)
            dve.wait_ge(s_xh, TT * (NORM_END + 1))
            dve.wait_ge(s_fgin, 16)
            for t in range(TT):
                V.tensor_tensor(XH[:, t, :], XH[:, t, :], fin_gain, ALU.mult).then_inc(s_fin, 1)


_INS = ["x", "mem", "rel_bias", "gains", "final_norm", "consts", "w_mem_kv", "w_out", "even_w_in", "even_w_gate",
        "even_w_up", "even_w_down", "odd_w_in", "odd_w_uk", "odd_w_uv", "odd_w_router", "odd_w_gate", "odd_w_up",
        "odd_w_down"]


def kernel(**inputs):
    import concourse.bacc as bacc
    from concourse.bass_utils import run_bass_kernel_spmd

    given = {k: np.ascontiguousarray(v) for k, v in inputs.items()}
    rows = [given["mem_norm"], given["mixer_norm"][0], given["ffn_norm"][0], given["mixer_norm"][1],
            given["ffn_norm"][1], given["odd_kv_norm"][0]]
    given["gains"] = np.ascontiguousarray(np.concatenate([r.reshape(-1, P) for r in rows]).T)
    given["consts"] = shape_constants()

    nc = bacc.Bacc("TRN2", target_bir_lowering=False, num_devices=1)
    arrays, args = {}, []
    for name in _INS:
        arrays[f"in_{name}"] = given[name]
        args.append(nc.dram_tensor(f"in_{name}", given[name].shape, mybir.dt.from_np(given[name].dtype),
                                   kind="ExternalInput").ap())
    args.append(nc.dram_tensor("out_0", (1, SEQ, D), F32, kind="ExternalOutput").ap())
    build(nc, *args)
    r = run_bass_kernel_spmd(nc, [arrays], core_ids=[0])
    return r.results[0]["out_0"]
```
